# Optimizing a Trainium2 kernel written in Bass

```python
import jax
import jax.numpy as jnp
from jax import lax
import numpy as np

D_MODEL = 1024
BATCH = 1
SEQ = 512
DEPTH = 1

EPS = 1e-6
SSD_HEADS = 8
SSD_HEAD_DIM = 64
SSD_WIDTH = SSD_HEADS * SSD_HEAD_DIM
SSD_GROUPS = 2
SSD_STATE = 128
SSD_CONV = 4
SSD_CHUNK = 128
SSD_CONV_DIM = SSD_WIDTH + 2 * SSD_GROUPS * SSD_STATE
MLA_HEADS = 8
MLA_Q_RANK = 256
MLA_KV_RANK = 128
MLA_NOPE = 64
MLA_ROPE = 32
MLA_V = 64
MLA_QK = MLA_NOPE + MLA_ROPE
MLA_WIDTH = MLA_HEADS * MLA_V
ROPE_THETA = 10000.0
ATTN_BLOCK = 128
MIX_WIDTH = SSD_WIDTH + MLA_WIDTH
IN_SPLITS = (SSD_WIDTH, SSD_CONV_DIM, SSD_HEADS, MLA_Q_RANK, MLA_KV_RANK, MLA_ROPE)
IN_WIDTH = SSD_WIDTH + SSD_CONV_DIM + SSD_HEADS + MLA_Q_RANK + MLA_KV_RANK + MLA_ROPE
N_EXPERTS = 32
TOP_K = 4
D_FF = 1024
SWIGLU_LIMIT = 7.0
SWIGLU_ALPHA = 1.702
MOE_BLOCK = 128

kernel_name = 'hybrid_ssd_mla_moe_layer'

def _split_points(widths):
    return tuple(int(v) for v in np.cumsum(widths)[:-1])

def rms_norm(x, g):
    xf = x.astype(jnp.float32)
    y = xf * lax.rsqrt(jnp.mean(xf * xf, axis=-1, keepdims=True) + EPS)
    return (y * g.astype(jnp.float32)).astype(x.dtype)

def causal_depthwise_conv(u, w, b):
    ch = u.shape[-1]
    out = lax.conv_general_dilated(
        u, w[:, None, :].astype(u.dtype), window_strides=(1,),
        padding=((SSD_CONV - 1, 0),), dimension_numbers=('NWC', 'WIO', 'NWC'),
        feature_group_count=ch)
    return out + b.astype(u.dtype)

def ssd_chunked(x, dt, a, b_in, c_in):
    bsz, seqlen, nh, hp = x.shape
    g, n = b_in.shape[2], b_in.shape[3]
    j = nh // g
    q = SSD_CHUNK
    nc = seqlen // q
    xd = (x * dt[..., None]).reshape(bsz, nc, q, g, j, hp)
    a_dt = (dt * a).reshape(bsz, nc, q, g, j)
    bc = b_in.reshape(bsz, nc, q, g, n)
    cc = c_in.reshape(bsz, nc, q, g, n)
    a_cum = jnp.cumsum(a_dt, axis=2)
    seg = a_cum[:, :, :, None] - a_cum[:, :, None, :]
    causal = jnp.tril(jnp.ones((q, q), dtype=bool))[None, None, :, :, None, None]
    decay = jnp.exp(jnp.where(causal, seg, -jnp.inf))
    scores = jnp.einsum('bclgn,bcsgn->bclsg', cc, bc)
    y_diag = jnp.einsum('bclsgj,bcsgjp->bclgjp', scores[..., None] * decay, xd)
    decay_to_end = jnp.exp(a_cum[:, :, -1:] - a_cum)
    states = jnp.einsum('bcsgn,bcsgj,bcsgjp->bcgjpn', bc, decay_to_end, xd)
    chunk_decay = jnp.exp(a_cum[:, :, -1])

    def step(h, inp):
        s_c, d_c = inp
        return h * d_c[..., None, None] + s_c, h

    h0 = jnp.zeros((bsz, g, j, hp, n), dtype=x.dtype)
    _, prev = lax.scan(step, h0, (jnp.swapaxes(states, 0, 1), jnp.swapaxes(chunk_decay, 0, 1)))
    prev = jnp.swapaxes(prev, 0, 1)
    y_off = jnp.einsum('bclgn,bcgjpn,bclgj->bclgjp', cc, prev, jnp.exp(a_cum))
    return (y_diag + y_off).reshape(bsz, seqlen, nh, hp)

def ssd_mixer(z, xbc, dt_raw, conv_w, conv_b, dt_bias, a_log, d_skip, norm_g):
    bsz, seqlen, _ = z.shape
    xbc = jax.nn.silu(causal_depthwise_conv(xbc, conv_w, conv_b))
    xs, bs, cs = jnp.split(xbc, _split_points((SSD_WIDTH, SSD_GROUPS * SSD_STATE, SSD_GROUPS * SSD_STATE)), axis=-1)
    xh = xs.reshape(bsz, seqlen, SSD_HEADS, SSD_HEAD_DIM).astype(jnp.float32)
    bm = bs.reshape(bsz, seqlen, SSD_GROUPS, SSD_STATE).astype(jnp.float32)
    cm = cs.reshape(bsz, seqlen, SSD_GROUPS, SSD_STATE).astype(jnp.float32)
    dt = jax.nn.softplus(dt_raw.astype(jnp.float32) + dt_bias.astype(jnp.float32))
    a = -jnp.exp(a_log.astype(jnp.float32))
    y = ssd_chunked(xh, dt, a, bm, cm) + d_skip.astype(jnp.float32)[:, None] * xh
    y = y.reshape(bsz, seqlen, SSD_WIDTH) * jax.nn.silu(z.astype(jnp.float32))
    yg = y.reshape(bsz, seqlen, SSD_GROUPS, SSD_WIDTH // SSD_GROUPS)
    yg = yg * lax.rsqrt(jnp.mean(yg * yg, axis=-1, keepdims=True) + EPS)
    y = yg.reshape(bsz, seqlen, SSD_WIDTH) * norm_g.astype(jnp.float32)
    return y.astype(z.dtype)

def rope_tables(positions):
    inv_freq = ROPE_THETA ** (-jnp.arange(0, MLA_ROPE, 2, dtype=jnp.float32) / MLA_ROPE)
    ang = positions.astype(jnp.float32)[..., None] * inv_freq
    return jnp.cos(ang), jnp.sin(ang)

def apply_rope(x, cos, sin):
    x1, x2 = jnp.split(x, 2, axis=-1)
    cos = cos.astype(x.dtype)
    sin = sin.astype(x.dtype)
    return jnp.concatenate([x1 * cos - x2 * sin, x2 * cos + x1 * sin], axis=-1)

def mla_mixer(c_q, c_kv, k_rope, positions, q_norm_g, w_uq, kv_norm_g, w_ukv):
    bsz, seqlen, _ = c_q.shape
    q = (rms_norm(c_q, q_norm_g) @ w_uq).reshape(bsz, seqlen, MLA_HEADS, MLA_QK)
    q_nope, q_rope = jnp.split(q, (MLA_NOPE,), axis=-1)
    kv = (rms_norm(c_kv, kv_norm_g) @ w_ukv).reshape(bsz, seqlen, MLA_HEADS, MLA_NOPE + MLA_V)
    k_nope, v = jnp.split(kv, (MLA_NOPE,), axis=-1)
    cos, sin = rope_tables(positions)
    q_rope = apply_rope(q_rope, cos[:, :, None, :], sin[:, :, None, :])
    k_rope = apply_rope(k_rope, cos, sin)
    scale = MLA_QK ** -0.5
    q_nope = q_nope * scale
    q_rope = q_rope * scale
    key_pos = jnp.arange(seqlen)

    def block(i):
        start = i * ATTN_BLOCK
        qn = lax.dynamic_slice_in_dim(q_nope, start, ATTN_BLOCK, axis=1)
        qr = lax.dynamic_slice_in_dim(q_rope, start, ATTN_BLOCK, axis=1)
        s = (jnp.einsum('bqhd,bkhd->bhqk', qn, k_nope)
             + jnp.einsum('bqhr,bkr->bhqk', qr, k_rope)).astype(jnp.float32)
        q_pos = start + jnp.arange(ATTN_BLOCK)
        mask = key_pos[None, :] <= q_pos[:, None]
        p = jax.nn.softmax(jnp.where(mask, s, -jnp.inf), axis=-1).astype(v.dtype)
        return jnp.einsum('bhqk,bkhd->bqhd', p, v)

    o = lax.map(block, jnp.arange(seqlen // ATTN_BLOCK))
    return jnp.transpose(o, (1, 0, 2, 3, 4)).reshape(bsz, seqlen, MLA_WIDTH)

def moe_ffn(h, w_router, b_router, w_gate_up, b_gate_up, w_down, b_down):
    bsz, seqlen, d = h.shape
    t = bsz * seqlen
    xf = h.reshape(t, d)
    logits = (xf @ w_router + b_router).astype(jnp.float32)
    top_vals, top_idx = lax.top_k(logits, TOP_K)
    gates = jax.nn.softmax(top_vals, axis=-1)
    na = t * TOP_K
    flat_e = top_idx.reshape(na).astype(jnp.int32)
    flat_tok = jnp.repeat(jnp.arange(t, dtype=jnp.int32), TOP_K)
    flat_w = gates.reshape(na)
    order = jnp.argsort(flat_e)
    sorted_e = flat_e[order]
    counts = jnp.zeros((N_EXPERTS,), jnp.int32).at[flat_e].add(1)
    padded = ((counts + MOE_BLOCK - 1) // MOE_BLOCK) * MOE_BLOCK
    start_unpad = jnp.cumsum(counts) - counts
    end_pad = jnp.cumsum(padded)
    start_pad = end_pad - padded
    dest = start_pad[sorted_e] + (jnp.arange(na, dtype=jnp.int32) - start_unpad[sorted_e])
    n_slots = na + N_EXPERTS * MOE_BLOCK
    n_blocks = n_slots // MOE_BLOCK
    slot_tok = jnp.full((n_slots,), t, jnp.int32).at[dest].set(flat_tok[order])
    slot_w = jnp.zeros((n_slots,), jnp.float32).at[dest].set(flat_w[order])
    block_start = jnp.arange(n_blocks, dtype=jnp.int32) * MOE_BLOCK
    block_e = jnp.minimum(jnp.sum(block_start[:, None] >= end_pad[None, :], axis=1), N_EXPERTS - 1)
    x_pad = jnp.concatenate([xf, jnp.zeros((1, d), xf.dtype)], axis=0)
    xs = x_pad[slot_tok].reshape(n_blocks, MOE_BLOCK, d)

    def expert_block(args):
        xb, e = args
        gu = xb @ w_gate_up[e] + b_gate_up[e]
        gate, up = jnp.split(gu, 2, axis=-1)
        gate = jnp.minimum(gate, SWIGLU_LIMIT)
        up = jnp.clip(up, -SWIGLU_LIMIT, SWIGLU_LIMIT)
        glu = gate * jax.nn.sigmoid(SWIGLU_ALPHA * gate)
        return ((up + 1.0) * glu) @ w_down[e] + b_down[e]

    ys = lax.map(expert_block, (xs, block_e)).reshape(n_slots, d)
    ys = ys * slot_w[:, None].astype(ys.dtype)
    out = jnp.zeros((t + 1, d), ys.dtype).at[slot_tok].add(ys)[:t]
    return out.reshape(bsz, seqlen, d)

def setup_inputs(seed: int = 0) -> dict:
    key = jax.random.key(seed)
    ks = jax.random.split(key, 32)
    f32 = jnp.float32

    def nrm(k, shape, scale):
        return jax.random.normal(k, shape, f32) * scale

    def gain(k, shape):
        return 1.0 + 0.02 * jax.random.normal(k, shape, f32)

    x = jax.random.normal(ks[0], (BATCH, SEQ, D_MODEL), f32)
    offsets = jax.random.randint(ks[1], (BATCH, 1), 0, 1024, dtype=jnp.int32)
    positions = jnp.arange(SEQ, dtype=jnp.int32)[None, :] + offsets
    dt0 = jnp.exp(jax.random.uniform(ks[6], (DEPTH, SSD_HEADS), f32, np.log(1e-3), np.log(1e-1)))
    dt_bias = dt0 + jnp.log(-jnp.expm1(-dt0))
    a_log = jnp.log(jax.random.uniform(ks[7], (DEPTH, SSD_HEADS), f32, 1.0, 16.0))
    return {
        'x': x,
        'positions': positions,
        'norm_mix_g': gain(ks[2], (DEPTH, D_MODEL)),
        'w_in': nrm(ks[3], (DEPTH, D_MODEL, IN_WIDTH), D_MODEL ** -0.5),
        'conv_w': nrm(ks[4], (DEPTH, SSD_CONV, SSD_CONV_DIM), SSD_CONV ** -0.5),
        'conv_b': nrm(ks[5], (DEPTH, SSD_CONV_DIM), 0.01),
        'dt_bias': dt_bias,
        'a_log': a_log,
        'd_skip': 1.0 + 0.1 * jax.random.normal(ks[8], (DEPTH, SSD_HEADS), f32),
        'ssd_norm_g': gain(ks[9], (DEPTH, SSD_WIDTH)),
        'q_norm_g': gain(ks[10], (DEPTH, MLA_Q_RANK)),
        'w_uq': nrm(ks[11], (DEPTH, MLA_Q_RANK, MLA_HEADS * MLA_QK), MLA_Q_RANK ** -0.5),
        'kv_norm_g': gain(ks[12], (DEPTH, MLA_KV_RANK)),
        'w_ukv': nrm(ks[13], (DEPTH, MLA_KV_RANK, MLA_HEADS * (MLA_NOPE + MLA_V)), MLA_KV_RANK ** -0.5),
        'w_out': nrm(ks[14], (DEPTH, MIX_WIDTH, D_MODEL), MIX_WIDTH ** -0.5),
        'norm_ffn_g': gain(ks[15], (DEPTH, D_MODEL)),
        'w_router': nrm(ks[16], (DEPTH, D_MODEL, N_EXPERTS), D_MODEL ** -0.5),
        'b_router': nrm(ks[17], (DEPTH, N_EXPERTS), 0.01),
        'w_gate_up': nrm(ks[18], (DEPTH, N_EXPERTS, D_MODEL, 2 * D_FF), D_MODEL ** -0.5),
        'b_gate_up': nrm(ks[19], (DEPTH, N_EXPERTS, 2 * D_FF), 0.01),
        'w_down': nrm(ks[20], (DEPTH, N_EXPERTS, D_FF, D_MODEL), D_FF ** -0.5),
        'b_down': nrm(ks[21], (DEPTH, N_EXPERTS, D_MODEL), 0.01),
        'norm_final_g': gain(ks[22], (D_MODEL,)),
    }

def reference(x, positions, norm_mix_g, w_in, conv_w, conv_b, dt_bias, a_log, d_skip, ssd_norm_g,
              q_norm_g, w_uq, kv_norm_g, w_ukv, w_out, norm_ffn_g, w_router, b_router,
              w_gate_up, b_gate_up, w_down, b_down, norm_final_g):
    for l in range(DEPTH):
        h = rms_norm(x, norm_mix_g[l])
        proj = h @ w_in[l]
        z, xbc, dt_raw, c_q, c_kv, k_rope = jnp.split(proj, _split_points(IN_SPLITS), axis=-1)
        y_ssd = ssd_mixer(z, xbc, dt_raw, conv_w[l], conv_b[l], dt_bias[l], a_log[l], d_skip[l], ssd_norm_g[l])
        y_mla = mla_mixer(c_q, c_kv, k_rope, positions, q_norm_g[l], w_uq[l], kv_norm_g[l], w_ukv[l])
        x = x + jnp.concatenate([y_ssd, y_mla], axis=-1) @ w_out[l]
        h = rms_norm(x, norm_ffn_g[l])
        x = x + moe_ffn(h, w_router[l], b_router[l], w_gate_up[l], b_gate_up[l], w_down[l], b_down[l])
    return rms_norm(x, norm_final_g)


_drawn_inputs = setup_inputs


def setup_inputs(seed=0):
    import zlib

    import numpy as np

    out = dict(_drawn_inputs(seed))
    spreads = {}
    factors = {'q_norm_g': 5.558,
     'kv_norm_g': 4.367,
     'b_gate_up': 28.949,
     'b_down': 33.265,
     'norm_final_g': 7.998,
     'conv_b': 5.873,
     'd_skip': 2.898,
     'ssd_norm_g': 7.172,
     'norm_ffn_g': 3.623,
     'b_router': 7.107}
    for name, (base, spread) in spreads.items():
        noise = np.random.default_rng([zlib.crc32(name.encode()), seed]).standard_normal(out[name].shape)
        drawn = base * np.exp(spread * noise) if base else spread * noise
        out[name] = jnp.asarray(drawn.astype(out[name].dtype))
    for name, factor in factors.items():
        out[name] = (out[name] * factor).astype(out[name].dtype)
    return out
```

```python
from contextlib import ExitStack

import numpy as np
import concourse.bass as bass
from concourse import mybir

F32 = mybir.dt.float32
F32R = mybir.dt.float32r
BF16 = mybir.dt.bfloat16
I32 = mybir.dt.int32
U32 = mybir.dt.uint32
ALU = mybir.AluOpType
ACT = mybir.ActivationFunctionType
AX = mybir.AxisListType.X

P = 128
SEQ, DM = 512, 1024
NT = SEQ // P
KD = DM // P
EPS = 1e-6
HEADS, HD, STATE, GROUPS = 8, 64, 128, 2
SSDW = HEADS * HD
QR, KVR, NOPE, ROPE, VD = 256, 128, 64, 32, 64
QK = NOPE + ROPE
SCALE = QK ** -0.5
NE, TOPK, DFF = 32, 4, 1024
LIMIT, ALPHA = 7.0, 1.702
NEG = -1e30
CHUNK = 2048
RAW, SPL = 4, 3
DVE_COLS = 1664
IN_CHUNKS, OUT_CHUNKS = 8, 4
N0 = IN_CHUNKS + OUT_CHUNKS
GUC, DNC = 8, 4
EC = GUC + DNC
PASS = NE * EC
SMALL = 424
PADE = NE + 2
TRASH = SEQ
TWO_PI = 6.283185307179586
C1 = 6.28125
C2 = float(np.float32(0.0019353071795864769))
C3 = float(TWO_PI - C1 - C2)
MAGIC = 12582912.0


def block_of(n):
    return (4 * SMALL, 1408) if n < 2 else (CHUNK, DVE_COLS)


MLA = [("lat", 0, "A"), ("lat", 1, "D"), ("lat", 2, "A"), ("kr", 0, "D"), ("kr", 1, "D"),
       ("qn", 0, "A"), ("qn", 1, "D"), ("qn", 2, "A"), ("qn", 3, "D"),
       ("qs", 0, "D"), ("qr", 0, "D"), ("qs", 1, "D"), ("qr", 1, "D"),
       ("kn", 0, "A"), ("kn", 1, "A"), ("kn", 2, "D"), ("kn", 3, "A"),
       ("v", 0, "A"), ("v", 1, "D"), ("v", 2, "A"), ("v", 3, "A")]
WQ = 10
NU = NT * HEADS


def layer(nc, A, out):
    with ExitStack() as ctx:
        base = nc.sbuf_base
        base = (base + 63) // 64 * 64

        def at(name, off, shape, dt=F32):
            return nc.alloc_sbuf_tensor_at(name, shape, dt, offset=base + off)

        def sem(name):
            return ctx.enter_context(nc.semaphore(name))

        raw = at("raw", 0, [P, RAW, CHUNK])
        whi = at("whi", 32768, [P, SPL, CHUNK], F32R)
        wlo = at("wlo", 57344, [P, SPL, CHUNK], F32R)
        RA, RF, RC, RD, RE, RG, RH, RI, RJ, RK = (81920, 114688, 131072, 147456, 155904, 164096,
                                                  172288, 190720, 194816, 198912)
        actT_hi = at("actT_hi", RA, [P, KD, SEQ], F32R)
        actT_lo = at("actT_lo", RA + 16384, [P, KD, SEQ], F32R)
        QT = at("QT", RA, [P, HEADS, SEQ])
        KT = at("KT", RA + 16384, [P, HEADS, SEQ])
        xnat = at("xnat", RF, [P, NT, DM])
        latn = at("latn", RF, [P, NT, QR + KVR])
        krn = at("krn", RF + 6144, [P, NT, 2, ROPE])
        Ynat = at("Ynat", RF, [P, NT, DM])
        h2 = at("h2", RF, [P, NT, DM])
        XBC = at("XBC", RC, [P, 8, SEQ])
        x2 = at("x2", RC, [P, NT, DM])
        U = at("U", RD, [P, 4, 3 + SEQ])
        Pr = at("Pr", RD, [P, 2, SEQ])
        PT = at("PT", RD + 4096, [P, 2, NT, P])
        Dm = at("Dm", RD, [P, GROUPS, 4, P])
        Mm = at("Mm", RD + 4096, [P, GROUPS, 4, P])
        h2T = at("h2T", RD, [P, 2, KD, P])
        sz = at("sz", RE, [P, NT, SSDW])
        V = at("V", RG, [P, NT, SSDW])
        Xn = at("Xn", RG, [P, NT, SSDW])
        wqn = at("wqn", RH, [P, 2, HEADS * NOPE])
        wqs = at("wqs", RH + 4096, [P, 2, HEADS * ROPE])
        wqr = at("wqr", RH + 6144, [P, 2, HEADS * ROPE])
        wkn = at("wkn", RH + 8192, [P, HEADS * NOPE])
        wv = at("wv", RH + 10240, [P, HEADS * VD])
        cqT = at("cqT", RH + 12288, [P, 2, SEQ])
        ckvT = at("ckvT", RH + 16384, [P, SEQ])
        Bn = at("Bn", RH, [P, 2, GROUPS, STATE])
        xd = at("xd", RH + 2048, [P, 2, SSDW])
        xdd = at("xdd", RH + 6144, [P, 2, SSDW])
        hst = at("hst", RH + 10240, [P, SSDW])
        htmp = at("htmp", RH + 12288, [P, SSDW])
        yt = at("yt", RH + 14336, [P, SSDW])
        ydx = at("ydx", RH + 16384, [P, SSDW])
        COS = at("COS", RI, [P, SEQ])
        SIN = at("SIN", RI + 2048, [P, SEQ])
        acc2 = at("acc2", RJ, [P, 2, SEQ])
        ropeS = at("ropeS", RJ, [P, SEQ])
        ropeR = at("ropeR", RJ + 2048, [P, SEQ])
        biasB = at("biasB", RE, [P, 3 * DFF], F32R)
        biasR = at("biasR", RE + 12288, [P, 3 * DFF])
        gffn = at("gffn", RE + 24576, [P, DM])
        gfin = at("gfin", RE + 28672, [P, DM])
        eq = at("eq", RI, [P, NT * TOPK, NE])
        eqg = at("eqg", RI + 2048, [P, NT * TOPK, NE])
        XT_hi = at("XT_hi", RA, [P, KD, P], F32R)
        XT_lo = at("XT_lo", RA + 4096, [P, KD, P], F32R)
        HT_hi = at("HT_hi", RA + 8192, [P, KD, P], F32R)
        HT_lo = at("HT_lo", RA + 12288, [P, KD, P], F32R)
        gc = at("gc", RA + 16384, [P, 2, 512])
        sg = at("sg", RA + 20480, [P, 2, 512])
        uc = at("uc", RA + 24576, [P, 2, 512])
        Xg = at("Xg", RA + 28672, [P, DM])
        ysb = at("ysb", RF, [P, DM])
        onehot = at("onehot", RF + 4096, [P, NT, P])
        sel_gu = at("sel_gu", RF + 6144, [P, P], F32R)
        sel_dn = at("sel_dn", RF + 6656, [P, P], F32R)
        fin = at("fin", RC, [P, NT, DM])
        fsq = at("fsq", RD, [P, DM])

        spot = [RK]

        def small(name, shape, dt=F32):
            n = int(np.prod(shape[1:])) * (2 if dt == BF16 else 4)
            t = at(name, spot[0], shape, dt)
            spot[0] += (n + 31) // 32 * 32
            return t

        ident = small("ident", [P, P])
        Uinc = small("Uinc", [P, P])
        onesf = small("onesf", [P, P])
        iota_f = small("iota_f", [P, P])
        Ustrict = at("Ustrict", RJ + 2560, [P, P])
        identb = small("identb", [P, P], BF16)
        maskA = small("maskA", [P, P], BF16)
        maskS = small("maskS", [P, P], BF16)
        vecT = small("vecT", [P, 64])
        esel = small("esel", [P, PADE])
        wrt = small("wrt", [P, KD, NE])
        brt = small("brt", [P, NE])
        dtb = small("dtb", [P, HEADS])
        alog = small("alog", [P, HEADS])
        dsk = small("dsk", [P, HEADS])
        dt = small("dt", [P, NT, HEADS])
        dtx = small("dtx", [P, NT, HEADS])
        adt = small("adt", [P, NT, HEADS])
        nacum = small("nacum", [P, NT, HEADS])
        eacum = small("eacum", [P, NT, HEADS])
        dte = small("dte", [P, NT, HEADS])
        cdec = small("cdec", [P, NT, HEADS])
        frq = small("frq", [P, 2])
        ss = small("ss", [P, 32])
        rstd = small("rstd", [P, 32])
        nmax = small("nmax", [P, 32])
        rsum = small("rsum", [P, 32])
        smid = small("smid", [P, 4])
        cntf = small("cntf", [P, 2])
        cnti = small("cnti", [P, 2], I32)
        idx_g = small("idx_g", [P, 1], I32)
        idx_s = small("idx_s", [P, 1], I32)
        idx_f = small("idx_f", [P, 1])
        vecs = at("vecs", RE + 4096, [55, P])
        posi = at("posi", RG, [P, SEQ], I32)
        posf = at("posf", RG + 2048, [P, SEQ])
        angk = at("angk", RG + 4096, [P, SEQ])
        ang = at("ang", RG + 6144, [P, SEQ])
        TG = at("TG", RJ, [P, NT, PADE, 3])
        rank = at("rank", RJ + 1664, [P, NT, PADE])
        lgt = at("lgt", RJ + 3104, [P, NT, NE])
        idxT = at("idxT", RJ + 3616, [P, PADE], I32)
        gwT = at("gwT", RJ + 3776, [P, PADE])
        mraw = small("mraw", [P, 32])
        mhalf = small("mhalf", [P, 4])
        krf = at("krf", RD + 4096, [ROPE, SEQ])
        junk = at("junk", RE, [P, 512])
        xjunk = at("xjunk", RC, [P, DM])
        x2junk = at("x2junk", RD, [P, DM])
        yjunk = at("yjunk", RI, [P, 256])
        kint = at("kint", RE + 2048, [P, P], I32)
        gsum = small("gsum", [P, NT])
        mask = small("mask", [P, NT, NE])
        top8 = small("top8", [P, NT, 8])
        topi = small("topi", [P, NT, 8], U32)
        topf = small("topf", [P, NT, TOPK])
        gate = small("gate", [P, NT, TOPK])
        assert base + spot[0] <= nc.sbuf_usable_end, (base + spot[0], nc.sbuf_usable_end)

        ps = ctx.enter_context(nc.psum_tensor("ps", [P, 8, 512], F32))

        acc_d = nc.dram_tensor("acc_rows", (SEQ + P, DM), F32).ap()
        h2_d = nc.dram_tensor("h2_rows", (SEQ, DM), F32).ap()

        names = """hi_done lo_dve lo_pool split_used vec_in par_in pos_in wq_in wr_in bias_in gn_in xr_in
            h2_out acc_out zero_out out_done konst_ok pad_ok iota_ok tg_ok vec_tr vec_ok xsq xs_ok x_tr
            hT_hi_ok hT_lo_ok lat_sq lat_ok u_ok conv_ok xbc_ok sz_ok dt_in dt_e adt_ok trig_in trig_ok
            mla_pe mla_act mla_dve kr_sum kr_act kr_dve s_done nm_done exp_done pt_done pt_act pt_dve pv_done
            ymla cum_pe cum_act cum_dve xb_tr xn_ok bn_ok xd_ok xdd_ok r_pe dm_ok mm_ok yd_pe yo_pe
            st_pe hm_ok h_ok y1_ok y2_ok ysq y_rms yssd yT_pe yT_hi yT_lo x2_ok x2sq h2_ok h2t_pe h2t_act
            lg_pe ge_in ge_ok mask_ok rank_pe route_ok bias_zero bias_hi bias_lo act_own dve_own pool_own
            oh_ok disp_pe disp_t idx_ok x_got xt_pe xt_hi xt_lo selg_ok seld_ok gub_pe gc_ok uc_ok sg_ok t_ok
            h_act ht_pe ht_hi ht_lo dnb_pe y_ok y_added rank_ok fsq_ok fo_ok x_rms lat_rms x2_rms f_rms rows_asked rows_sent""".split()
        (hi_done, lo_dve, lo_pool, split_used, vec_in, par_in, pos_in, wq_in, wr_in, bias_in, gn_in, xr_in,
         h2_out, acc_out, zero_out, out_done, konst_ok, pad_ok, iota_ok, tg_ok, vec_tr, vec_ok, xsq, xs_ok, x_tr,
         hT_hi_ok, hT_lo_ok, lat_sq, lat_ok, u_ok, conv_ok, xbc_ok, sz_ok, dt_in, dt_e, adt_ok, trig_in, trig_ok,
         mla_pe, mla_act, mla_dve, kr_sum, kr_act, kr_dve, s_done, nm_done, exp_done, pt_done, pt_act, pt_dve, pv_done,
         ymla, cum_pe, cum_act, cum_dve, xb_tr, xn_ok, bn_ok, xd_ok, xdd_ok, r_pe, dm_ok, mm_ok, yd_pe, yo_pe,
         st_pe, hm_ok, h_ok, y1_ok, y2_ok, ysq, y_rms, yssd, yT_pe, yT_hi, yT_lo, x2_ok, x2sq, h2_ok, h2t_pe, h2t_act,
         lg_pe, ge_in, ge_ok, mask_ok, rank_pe, route_ok, bias_zero, bias_hi, bias_lo, act_own, dve_own, pool_own,
         oh_ok, disp_pe, disp_t, idx_ok, x_got, xt_pe, xt_hi, xt_lo, selg_ok, seld_ok, gub_pe, gc_ok, uc_ok, sg_ok, t_ok,
         h_act, ht_pe, ht_hi, ht_lo, dnb_pe, y_ok, y_added, rank_ok, fsq_ok, fo_ok, x_rms, lat_rms, x2_rms, f_rms, rows_asked, rows_sent) = (sem(n) for n in names)
        raw_in = [sem(f"raw_in{k}") for k in range(RAW)]
        x_in = [sem(f"x_in{j}") for j in range(NT)]
        fin_in = [sem(f"fin_in{j}") for j in range(NT)]

        block = ctx.enter_context(nc.Block())

        w_in, w_out = A["w_in"][0], A["w_out"][0]
        w_gu = A["w_gate_up"][0].rearrange("e (k p) n -> e k p n", p=P)
        w_dn = A["w_down"][0].rearrange("e (c k p) n -> e c p k n", p=P, k=2)

        IN_COLS = [(SSDW + 2 * SSDW, SMALL), (SSDW, SSDW), (2 * SSDW, SSDW), (0, SSDW)]

        class Chain:

            def __init__(self, eng, s):
                self.eng, self.s, self.n = eng, s, 0

            def __call__(self, ins):
                ins.then_inc(self.s, 1)
                self.n += 1
                self.eng.wait_ge(self.s, self.n)

        def past(n):
            return n + 1

        def heads(t, n):
            return t.unsqueeze(2).to_broadcast([P, HEADS, n])

        def mla_evacuated(eng, i):
            mine = sum(1 for v in range(i + 1) if MLA[v][2] == MLA[i][2])
            eng.wait_ge(mla_act if MLA[i][2] == "A" else mla_dve, mine)

        def passes(eng, one_pass, first=0):
            eng.wait_ge(route_ok, 1)
            with eng.Fori(first, SEQ // P) as r:
                most = eng.value_load(cnti[0:1, 0:1], min_val=0, max_val=SEQ)
                with eng.If(most > r * P):
                    one_pass(r)

        @block.sync
        def _(sp):
            for j in range(NT):
                sp.dma_start(xnat[:, j, :], A["x"][0, j * P:(j + 1) * P, :]).then_inc(x_in[j], 16)

            def load(slot, src, free, width=CHUNK, k=1):
                if free is not None:
                    sp.wait_ge(lo_dve, free)
                    sp.wait_ge(lo_pool, free)
                sp.dma_start(raw[:, slot, 0:width].rearrange("p (k n) -> p k n", k=k), src).then_inc(raw_in[slot], 16)

            for n in range(IN_CHUNKS):
                c0, w = IN_COLS[n // 2]
                rows = w_in[(n % 2) * 4 * P:(n % 2 + 1) * 4 * P, c0:c0 + w].rearrange("(k p) n -> p k n", p=P)
                load(n % RAW, rows, n - RAW + 1 if n >= RAW else None, 4 * w, 4)
            for c in range(OUT_CHUNKS):
                n = IN_CHUNKS + c
                rows = w_out[2 * c * P:2 * (c + 1) * P, :].rearrange("(k p) n -> p k n", p=P)
                load(n % RAW, rows, n - RAW + 1, CHUNK, 2)

            def gate_up(e, n0, k0):
                for c in range(GUC):
                    load((k0 + c) % RAW, w_gu[bass.ds(e, 1), c].rearrange("a p n -> p a n"), n0 + (k0 + c - RAW + 1))

            def down(e, n0, k0):
                for c in range(DNC):
                    load((k0 + c) % RAW, w_dn[bass.ds(e, 1), c].rearrange("a p k n -> p (a k) n"),
                         n0 + (k0 + c - RAW + 1), CHUNK, 2)

            def one_pass(r):
                gate_up(0, r * PASS, N0)
                with sp.Fori(1, NE) as e:
                    n0 = r * PASS + e * EC
                    gate_up(e, n0, N0 + GUC - EC)
                    down(e - 1, n0, N0 + 2 * GUC - EC)
                down(NE - 1, r * PASS, N0 + PASS - DNC)

            one_pass(0)
            passes(sp, one_pass, first=1)

        @block.tensor
        def _(pe):
            T = nc.tensor

            def high_ready(n):
                pe.wait_ge(hi_done, n + 1)

            def low_ready(n):
                pe.wait_ge(lo_dve, n + 1)
                pe.wait_ge(lo_pool, n + 1)

            pe.wait_ge(konst_ok, 1)
            pe.wait_ge(vec_in, 6 * 16)
            T.transpose(ps[:, 7, 0:55], vecs[:, :], ident[0:55, 0:55]).then_inc(vec_tr, 1)
            pe.wait_ge(vec_ok, 1)
            for j in range(NT):
                pe.wait_ge(xs_ok, j + 1)
                for k in range(KD):
                    ins = T.transpose(ps[:, k, j * P:(j + 1) * P], xnat[:, j, k * P:(k + 1) * P], ident[:, :])
            ins.then_inc(x_tr, 1)

            for b in range(4):
                w = IN_COLS[b][1]
                bank0 = 4 * (b % 2)
                if b == 2:
                    pe.wait_ge(lat_sq, 2 * NT)
                    pe.wait_ge(lat_ok, NT)
                if b == 3:
                    pe.wait_ge(u_ok, 4)
                for half in range(2):
                    n = 2 * b + half
                    Wh = whi[:, n % SPL, 0:4 * w].rearrange("p (k n) -> p k n", k=4)
                    Wl = wlo[:, n % SPL, 0:4 * w].rearrange("p (k n) -> p k n", k=4)
                    if b == 0:
                        pe.wait_ge(hT_hi_ok, 8)
                        pe.wait_ge(hT_lo_ok, 8)
                    high_ready(n)
                    low_ready(n)
                    for kk in range(4):
                        k = 4 * half + kk
                        ah, al = actT_hi[:, k, :], actT_lo[:, k, :]
                        for m in range(4):
                            tm = slice(m * P, (m + 1) * P)
                            if b in (0, 3):
                                trio = ((ah[:, tm], Wh[:, kk, :]), (al[:, tm], Wh[:, kk, :]), (ah[:, tm], Wl[:, kk, :]))
                            else:
                                trio = ((Wh[:, kk, tm], ah), (Wh[:, kk, tm], al), (Wl[:, kk, tm], ah))
                            for q, (l, r) in enumerate(trio):
                                ins = T.matmul(ps[:, bank0 + m, 0:w], l, r, start=k == 0 and q == 0, stop=k == 7 and q == 2)
                    ins.then_inc(split_used, 1)

            for i, (kind, a, _) in enumerate(MLA):
                o = ps[:, i % 8, :]
                if i < 4:
                    pe.wait_ge(u_ok, 5 + i)
                elif i < 8:
                    pe.wait_ge(sz_ok, i - 3)
                else:
                    mla_evacuated(pe, i - 8)
                if kind == "lat":
                    for j in range(NT):
                        ins = T.transpose(o[:, j * P:(j + 1) * P], latn[:, j, a * P:(a + 1) * P], ident[:, :])
                elif kind == "kr":
                    for j in range(NT):
                        ins = T.transpose(o[0:ROPE, j * P:(j + 1) * P], krn[:, j, a, :], ident[:, :])
                elif kind in ("qn", "qs", "qr"):
                    if i == 5:
                        pe.wait_ge(wq_in, 16 * WQ)
                        mla_evacuated(pe, 0)
                        mla_evacuated(pe, 1)
                    for kk in range(2):
                        l = {"qn": wqn, "qs": wqs, "qr": wqr}[kind][:, kk, a * P:(a + 1) * P]
                        ins = T.matmul(o, l, cqT[:, kk, :], start=kk == 0, stop=kk == 1)
                elif kind == "kn":
                    mla_evacuated(pe, 2)
                    ins = T.matmul(o, wkn[:, a * P:(a + 1) * P], ckvT[:, :], start=True, stop=True)
                else:
                    ins = T.matmul(o, ckvT[:, a * P:(a + 1) * P], wv[:, :], start=True, stop=True)
                ins.then_inc(mla_pe, 1)
            for i in range(len(MLA) - 8, len(MLA)):
                mla_evacuated(pe, i)
            pe.wait_ge(kr_act, 1)
            pe.wait_ge(kr_dve, 1)

            def scores(u):
                i, h = u // HEADS, u % HEADS
                w = (i + 1) * P
                if u >= 2:
                    pe.wait_ge(exp_done, u - 1)
                if i:
                    T.matmul(ps[:, u % 2, 0:i * P], QT[0:QK, h, i * P:w], KT[0:QK, h, 0:i * P], start=True, stop=True)
                T.matmul(ps[:, u % 2, i * P:w], QT[0:QK, h, i * P:w], KT[0:QK, h, i * P:w], start=True, stop=False)
                T.matmul(ps[:, u % 2, i * P:w], identb[:, :], maskA[:, :], start=False, stop=True).then_inc(s_done, 1)

            def pt_copied(u):
                pe.wait_ge(pt_act if u % 2 else pt_dve, u // 2 + 1)

            def outputs(u):
                i, h = u // HEADS, u % HEADS
                pt_copied(u)
                if h == 0 and i >= 2:
                    pe.wait_ge(ymla, i - 1)
                for kk in range(i + 1):
                    ins = T.matmul(ps[:, 4 + i % 2, h * VD:(h + 1) * VD], PT[:, u % 2, kk, :],
                                   V[:, kk, h * VD:(h + 1) * VD], start=kk == 0, stop=kk == i)
                ins.then_inc(pv_done, 1)

            scores(0)
            scores(1)
            for u in range(NU):
                pe.wait_ge(exp_done, u + 1)
                if u >= 2:
                    pt_copied(u - 2)
                for kk in range(u // HEADS + 1):
                    ins = T.transpose(ps[:, 2 + u % 2, kk * P:(kk + 1) * P], Pr[:, u % 2, kk * P:(kk + 1) * P], ident[:, :])
                ins.then_inc(pt_done, 1)
                if u + 2 < NU:
                    scores(u + 2)
                if u >= 1:
                    outputs(u - 1)
            outputs(NU - 1)

            pe.wait_ge(adt_ok, 1)
            flat = adt[:, :, :].rearrange("p j h -> p (j h)")
            T.matmul(ps[:, 7, 0:32], Uinc[:, :], flat, start=True, stop=True)
            T.matmul(ps[:, 7, 32:64], onesf[:, :], flat, start=True, stop=True).then_inc(cum_pe, 1)
            pe.wait_ge(ymla, 3)
            pe.wait_ge(xbc_ok, 8)
            for j in range(NT):
                tj = slice(j * P, (j + 1) * P)
                if j >= 1:
                    pe.wait_ge(xn_ok, j)
                    pe.wait_ge(bn_ok, j)
                    pe.wait_ge(mm_ok, 2 * j)
                for m in range(4):
                    T.transpose(ps[:, 0, m * P:(m + 1) * P], XBC[:, m, tj], ident[:, :])
                for g in range(GROUPS):
                    T.transpose(ps[:, 1, g * P:(g + 1) * P], XBC[:, 4 + g, tj], ident[:, :])
                for g in range(GROUPS):
                    ins = T.matmul(ps[:, 1, (2 + g) * P:(3 + g) * P], XBC[:, 4 + g, tj], XBC[:, 6 + g, tj],
                                   start=True, stop=True)
                ins.then_inc(xb_tr, 1)
                for g in range(GROUPS):
                    if j >= 1:
                        pe.wait_ge(dm_ok, 2 * (j - 1) + g + 1)
                    for q in range(4):
                        o = ps[:, 2 + g, q * P:(q + 1) * P]
                        h = 4 * g + q
                        T.matmul(o, adt[:, j, h:h + 1].to_broadcast([P, P]), Uinc[:, :], start=True, stop=False)
                        ins = T.matmul(o, identb[:, :], maskS[:, :], start=False, stop=True)
                    ins.then_inc(r_pe, 1)
                if j >= 1:
                    pe.wait_ge(h_ok, j)
                    if j >= 2:
                        pe.wait_ge(y1_ok, j)
                    for g in range(GROUPS):
                        ins = T.matmul(ps[:, 6, g * 256:(g + 1) * 256], XBC[:, 6 + g, tj],
                                       hst[:, g * 256:(g + 1) * 256], start=True, stop=True)
                    ins.then_inc(yo_pe, 1)
                pe.wait_ge(xd_ok, j + 1)
                if j == 1:
                    pe.wait_ge(ymla, 4)
                if j >= 2:
                    pe.wait_ge(y1_ok, j - 1)
                for g in range(GROUPS):
                    pe.wait_ge(mm_ok, 2 * j + g + 1)
                    for q in range(4):
                        h = 4 * g + q
                        ins = T.matmul(ps[:, 4 + j % 2, h * HD:(h + 1) * HD], Mm[:, g, q, :],
                                       xd[:, j % 2, h * HD:(h + 1) * HD], start=True, stop=True)
                ins.then_inc(yd_pe, 1)
                if j < NT - 1:
                    pe.wait_ge(xdd_ok, j + 1)
                    pe.wait_ge(bn_ok, j + 1)
                    if j == 0:
                        pe.wait_ge(cum_dve, 2)
                        pe.wait_ge(cum_act, 2)
                    for g in range(GROUPS):
                        ins = T.matmul(ps[:, 7, g * 256:(g + 1) * 256], Bn[:, j % 2, g, :],
                                       xdd[:, j % 2, g * 256:(g + 1) * 256], start=True, stop=True)
                    ins.then_inc(st_pe, 1)

            pe.wait_ge(y1_ok, NT)
            for f in (4, 5, 6, 7, 0, 1, 2, 3):
                if f == 0:
                    pe.wait_ge(yssd, NT)
                for j in range(NT):
                    ins = T.transpose(ps[:, f, j * P:(j + 1) * P], Ynat[:, j, f * P:(f + 1) * P], ident[:, :])
                ins.then_inc(yT_pe, 1)
            pe.wait_ge(yT_hi, KD)
            pe.wait_ge(yT_lo, KD)
            for c in range(OUT_CHUNKS):
                n = IN_CHUNKS + c
                Wh = whi[:, n % SPL, :].rearrange("p (k n) -> p k n", k=2)
                Wl = wlo[:, n % SPL, :].rearrange("p (k n) -> p k n", k=2)
                high_ready(n)
                low_ready(n)
                for kk in range(2):
                    k = 2 * c + kk
                    for j in range(NT):
                        for q, (l, W) in enumerate(((actT_hi, Wh), (actT_lo, Wh), (actT_hi, Wl))):
                            for f in range(2):
                                ins = T.matmul(ps[:, 2 * j + f, :], l[:, k, j * P:(j + 1) * P],
                                               W[:, kk, f * 512:(f + 1) * 512], start=k == 0 and q == 0, stop=k == 7 and q == 2)
                ins.then_inc(split_used, 1)

            for j in range(NT):
                pe.wait_ge(h2_ok, j + 1)
                for k in range(KD):
                    ins = T.transpose(ps[:, 2 * j + k // 4, (k % 4) * P:(k % 4 + 1) * P], h2[:, j, k * P:(k + 1) * P], ident[:, :])
                ins.then_inc(h2t_pe, 1)
            pe.wait_ge(wr_in, 32)
            for j in range(NT):
                pe.wait_ge(h2t_act, j + 1)
                for k in range(KD):
                    ins = T.matmul(ps[:, 2 * j, 0:NE], h2T[:, j % 2, k, :], wrt[:, k, :], start=k == 0, stop=k == KD - 1)
                ins.then_inc(lg_pe, 1)
            pe.wait_ge(mask_ok, 1)
            pe.wait_ge(tg_ok, 2)
            for j in range(NT):
                for i in range(j + 1):
                    T.matmul(ps[:, 1, j * NE:(j + 1) * NE], Ustrict[:, :] if i == j else onesf[:, :], mask[:, i, :],
                             start=i == 0, stop=i == j)
            for i in range(NT):
                ins = T.matmul(ps[:, 3, 0:NE], onesf[:, :], mask[:, i, :], start=i == 0, stop=i == NT - 1)
            ins.then_inc(rank_pe, 1)

            def dispatch(D, e):
                pe.wait_ge(oh_ok, D + 1)
                for j in range(NT):
                    ins = T.matmul(ps[:, 6, 0:3], onehot[:, j, :], TG[:, j, bass.ds(e, 1), :].rearrange("p a c -> p (a c)"),
                                   start=j == 0, stop=j == NT - 1)
                ins.then_inc(disp_pe, 1)

            def rows(D, tables):
                pe.wait_ge(x_got, 16 * (D + 1))
                pe.wait_ge(idx_ok, tables)
                for k in range(KD):
                    ins = T.transpose(ps[:, 6 + k // 4, (k % 4) * P:(k % 4 + 1) * P], Xg[:, k * P:(k + 1) * P], ident[:, :])
                ins.then_inc(xt_pe, 1)

            def gate_up(E, X, D, e, n0, k0):
                pe.wait_ge(selg_ok, E + 1)
                pe.wait_ge(uc_ok, past(2 * E))
                for m in range(4):
                    ins = T.matmul(ps[:, m, :], sel_gu[:, :], biasB[:, m * 512:(m + 1) * 512], start=True, stop=False)
                ins.then_inc(gub_pe, 1)
                pe.wait_ge(xt_hi, X + 1)
                pe.wait_ge(xt_lo, X + 1)
                for c in range(GUC):
                    if c == 4:
                        pe.wait_ge(ht_hi, past(E))
                        pe.wait_ge(ht_lo, past(E))
                        dispatch(D + 2, e + 2)
                    s = (k0 + c) % SPL
                    high_ready(n0 + (k0 + c))
                    for l in (XT_hi, XT_lo):
                        for m in range(4):
                            T.matmul(ps[:, m, :], l[:, c, :], whi[:, s, m * 512:(m + 1) * 512], start=False, stop=False)
                    low_ready(n0 + (k0 + c))
                    for m in range(4):
                        ins = T.matmul(ps[:, m, :], XT_hi[:, c, :], wlo[:, s, m * 512:(m + 1) * 512],
                                       start=False, stop=c == GUC - 1)
                    ins.then_inc(split_used, 1)

            def down(E, n0, k0):
                pe.wait_ge(seld_ok, E + 1)
                pe.wait_ge(y_ok, past(E))
                for m in range(2):
                    ins = T.matmul(ps[:, 4 + m, :], sel_dn[:, :], biasB[:, (4 + m) * 512:(5 + m) * 512], start=True, stop=False)
                ins.then_inc(dnb_pe, 1)
                pe.wait_ge(ht_hi, past(E + 1))
                pe.wait_ge(ht_lo, past(E + 1))
                for c in range(DNC):
                    s = (k0 + c) % SPL
                    high_ready(n0 + (k0 + c))
                    for kk in range(2):
                        for l in (HT_hi, HT_lo):
                            for m in range(2):
                                T.matmul(ps[:, 4 + m, :], l[:, 2 * c + kk, :],
                                         whi[:, s, kk * DM + m * 512:kk * DM + (m + 1) * 512], start=False, stop=False)
                    low_ready(n0 + (k0 + c))
                    for kk in range(2):
                        for m in range(2):
                            ins = T.matmul(ps[:, 4 + m, :], HT_hi[:, 2 * c + kk, :],
                                           wlo[:, s, kk * DM + m * 512:kk * DM + (m + 1) * 512],
                                           start=False, stop=c == DNC - 1 and kk == 1)
                    ins.then_inc(split_used, 1)

            def hidden(E, X):
                pe.wait_ge(h_act, 2 * E + 2)
                pe.wait_ge(xt_hi, X)
                pe.wait_ge(xt_lo, X)
                for k in range(KD):
                    ins = T.transpose(ps[:, 6 + k // 4, (k % 4) * P:(k % 4 + 1) * P],
                                      uc[:, k // 4, (k % 4) * P:(k % 4 + 1) * P], ident[:, :])
                ins.then_inc(ht_pe, 1)

            pe.wait_ge(bias_lo, 1)

            def one_pass(r):
                E0, X0, D0 = r * NE, r * (NE + 1), r * PADE
                pe.wait_ge(ht_hi, past(E0))
                pe.wait_ge(ht_lo, past(E0))
                dispatch(D0, 0)
                rows(D0, D0 + 1)
                pe.wait_ge(xt_hi, X0 + 1)
                pe.wait_ge(xt_lo, X0 + 1)
                dispatch(D0 + 1, 1)
                pe.wait_ge(idx_ok, D0 + 2)
                gate_up(E0, X0, D0, 0, r * PASS, N0)
                rows(D0 + 1, D0 + 3)
                hidden(E0, X0 + 2)
                with pe.Fori(1, NE) as e:
                    E, X, D, n0 = E0 + e, X0 + e, D0 + e, r * PASS + e * EC
                    gate_up(E, X, D, e, n0, N0 + GUC - EC)
                    rows(D + 1, D + 3)
                    down(E - 1, n0, N0 + 2 * GUC - EC)
                    hidden(E, X + 2)
                down(E0 + (NE - 1), r * PASS, N0 + PASS - DNC)

            passes(pe, one_pass)

        @block.scalar
        def _(act):
            S = nc.scalar
            rows_of = lambda t: t.rearrange("(k p) -> k p", p=P)
            act.dma_start(vecs[0:8, :], rows_of(A["norm_mix_g"][0])).then_inc(vec_in, 16)
            act.dma_start(vecs[8:40, :], A["conv_w"][0].rearrange("w (k p) -> (w k) p", p=P)).then_inc(vec_in, 16)
            act.dma_start(vecs[40:48, :], rows_of(A["conv_b"][0])).then_inc(vec_in, 16)
            act.dma_start(vecs[48:50, :], rows_of(A["q_norm_g"][0])).then_inc(vec_in, 16)
            act.dma_start(vecs[50:51, :], rows_of(A["kv_norm_g"][0])).then_inc(vec_in, 16)
            act.dma_start(vecs[51:55, :], rows_of(A["ssd_norm_g"][0])).then_inc(vec_in, 16)
            act.dma_start(posi[:, :], A["positions"][0].partition_broadcast(P)).then_inc(pos_in, 16)
            act.dma_start(frq[:, :], A["rope_freq"]).then_inc(pos_in, 16)
            act.dma_start(dtb[:, :], A["dt_bias"][0].partition_broadcast(P)).then_inc(par_in, 16)
            act.dma_start(alog[:, :], A["a_log"][0].partition_broadcast(P)).then_inc(par_in, 16)
            act.dma_start(dsk[:, :], A["d_skip"][0].partition_broadcast(P)).then_inc(par_in, 16)
            per_head = lambda t: t.rearrange("p (h d) -> p h d", h=HEADS)
            for k in range(2):
                uq = per_head(A["w_uq"][0][k * P:(k + 1) * P, :])
                act.dma_start(per_head(wqn[:, k, :]), uq[:, :, 0:NOPE]).then_inc(wq_in, 16)
                act.dma_start(per_head(wqs[:, k, :]), uq[:, :, NOPE:QK]).then_inc(wq_in, 16)
                act.dma_start(per_head(wqr[:, k, :])[:, :, 0:ROPE // 2], uq[:, :, NOPE + ROPE // 2:QK]).then_inc(wq_in, 16)
                act.dma_start(per_head(wqr[:, k, :])[:, :, ROPE // 2:ROPE], uq[:, :, NOPE:NOPE + ROPE // 2]).then_inc(wq_in, 16)
            ukv = per_head(A["w_ukv"][0])
            act.dma_start(per_head(wkn[:, :]), ukv[:, :, 0:NOPE]).then_inc(wq_in, 16)
            act.dma_start(per_head(wv[:, :]), ukv[:, :, NOPE:NOPE + VD]).then_inc(wq_in, 16)
            act.dma_start(wrt[:, :, :], A["w_router"][0].rearrange("(k p) n -> p k n", p=P)).then_inc(wr_in, 16)
            act.dma_start(brt[:, :], A["b_router"][0].partition_broadcast(P)).then_inc(wr_in, 16)

            def high(n):
                if n >= SPL:
                    act.wait_ge(split_used, n - SPL + 1)
                act.wait_ge(raw_in[n % RAW], 16 * (n // RAW + 1))
                w = block_of(n)[0]
                S.activation(whi[:, n % SPL, 0:w], raw[:, n % RAW, 0:w], ACT.Copy).then_inc(hi_done, 1)

            for j in range(NT):
                act.wait_ge(x_in[j], 16)
                if j:
                    act.wait_ge(xsq, j)
                S.activation(xjunk[:, :], xnat[:, j, :], ACT.Square, accum_out=ss[:, j:j + 1]).then_inc(xsq, 1)
            act.wait_ge(vec_tr, 1)
            S.activation(vecT[:, 0:55], ps[:, 7, 0:55], ACT.Copy).then_inc(vec_ok, 1)
            for n in range(3):
                high(n)
            act.wait_ge(vec_ok, 1)
            act.wait_ge(x_tr, 1)
            for k in range(KD):
                S.activation(actT_hi[:, k, :], ps[:, k, :], ACT.Copy, scale=vecT[:, k:k + 1]).then_inc(hT_hi_ok, 1)
            act.wait_ge(trig_in, 2)
            S.activation(COS[:, :], ang[:, :], ACT.Sin)
            S.activation(SIN[:, :], angk[:, :], ACT.Sin, scale=frq[:, 1:2]).then_inc(trig_ok, 1)
            high(3)
            high(4)
            act.wait_ge(split_used, 2)
            for j in range(NT):
                if j:
                    act.wait_ge(lat_sq, 2 * j)
                S.activation(junk[:, 0:QR], ps[:, j, 8:8 + QR], ACT.Square, accum_out=ss[:, 4 + j:5 + j]).then_inc(lat_sq, 1)
                S.activation(junk[:, QR:QR + KVR], ps[:, j, 8 + QR:8 + QR + KVR], ACT.Square,
                             accum_out=ss[:, 8 + j:9 + j]).then_inc(lat_sq, 1)
            act.wait_ge(dt_in, 1)
            S.activation(dtx[:, :, :], dt[:, :, :], ACT.Abs).then_inc(dt_e, 1)
            act.wait_ge(dt_e, 1)
            S.activation(dtx[:, :, :], dtx[:, :, :], ACT.Exp, scale=-1.0).then_inc(dt_e, 1)
            act.wait_ge(par_in, 48)
            S.activation(alog[:, :], alog[:, :], ACT.Exp)
            act.wait_ge(dt_e, 2)
            S.activation(dtx[:, :, :], dtx[:, :, :], ACT.Ln, bias=1.0).then_inc(dt_e, 1)
            high(5)

            def window(m):
                if m >= 4:
                    act.wait_ge(conv_ok, m - 3)
                S.activation(U[:, m % 4, 3:3 + SEQ], ps[:, (4 if m < 4 else 0) + m % 4, :], ACT.Copy).then_inc(u_ok, 1)

            def channels(m):
                act.wait_ge(conv_ok, m + 1)
                S.activation(XBC[:, m, :], acc2[:, m % 2, :], ACT.Silu, bias=vecT[:, 40 + m:41 + m]).then_inc(xbc_ok, 1)

            act.wait_ge(split_used, 4)
            for m in range(4):
                window(m)
            high(6)
            for m in range(4):
                channels(m)
            high(7)
            act.wait_ge(split_used, 6)
            for m in range(4, 8):
                window(m)
            high(8)
            for m in range(4, 8):
                channels(m)
            act.wait_ge(split_used, 8)
            for j in range(NT):
                S.activation(sz[:, j, :], ps[:, 4 + j, :], ACT.Silu).then_inc(sz_ok, 1)
            high(9)
            high(10)

            for i, (kind, a, eng) in enumerate(MLA):
                if eng != "A":
                    continue
                b = i % 8
                act.wait_ge(mla_pe, i + 1)
                if kind == "lat":
                    dst = cqT[:, a, :] if a < 2 else ckvT[:, :]
                    S.activation(dst, ps[:, b, :], ACT.Copy, scale=vecT[:, 48 + a:49 + a]).then_inc(mla_act, 1)
                elif kind in ("qn", "kn"):
                    dst = QT if kind == "qn" else KT
                    S.activation(dst[0:NOPE, 2 * a, :], ps[0:NOPE, b, :], ACT.Copy)
                    S.activation(dst[0:NOPE, 2 * a + 1, :], ps[NOPE:P, b, :], ACT.Copy).then_inc(mla_act, 1)
                else:
                    S.activation(V[:, a, :], ps[:, b, :], ACT.Copy).then_inc(mla_act, 1)
            act.wait_ge(kr_sum, 1)
            for h in range(4, HEADS):
                ins = S.activation(KT[NOPE:QK, h, :], krf[:, :], ACT.Copy)
            ins.then_inc(kr_act, 1)

            def pt_copy(u):
                act.wait_ge(pt_done, u + 1)
                if u >= 2:
                    act.wait_ge(pv_done, u - 1)
                n = u // HEADS + 1
                S.activation(PT[:, u % 2, 0:n, :].rearrange("p k n -> p (k n)"), ps[:, 2 + u % 2, 0:n * P], ACT.Copy).then_inc(pt_act, 1)

            for u in range(NU):
                w = (u // HEADS + 1) * P
                act.wait_ge(nm_done, u + 1)
                if u >= 2:
                    act.wait_ge(pt_done, u - 1)
                S.activation(Pr[:, u % 2, 0:w], ps[:, u % 2, 0:w], ACT.Exp, bias=nmax[:, u:u + 1], scale=SCALE,
                             accum_out=rsum[:, u:u + 1]).then_inc(exp_done, 1)
                if u % 2 == 0 and u >= 2:
                    pt_copy(u - 1)
            pt_copy(NU - 1)

            fl = lambda t: t[:, :, :].rearrange("p j h -> p (j h)")
            act.wait_ge(cum_dve, 2)
            S.activation(fl(eacum), fl(nacum), ACT.Exp, scale=-1.0).then_inc(cum_act, 1)
            S.activation(fl(cdec), ps[:, 7, 32:64], ACT.Exp).then_inc(cum_act, 1)
            S.activation(fl(dte), fl(dtx), ACT.Exp).then_inc(cum_act, 1)

            def finish_y(j):
                act.wait_ge(y2_ok, j + 1)
                for g in range(GROUPS):
                    if 2 * j + g:
                        act.wait_ge(ysq, 2 * j + g)
                    S.activation(yjunk[:, :], Ynat[:, j, g * 256:(g + 1) * 256], ACT.Square,
                                 accum_out=ss[:, 20 + 2 * j + g:21 + 2 * j + g]).then_inc(ysq, 1)
                act.wait_ge(y_rms, j + 1)
                for g in range(GROUPS):
                    ins = S.activation(Ynat[:, j, g * 256:(g + 1) * 256], Ynat[:, j, g * 256:(g + 1) * 256], ACT.Copy,
                                       scale=rstd[:, 20 + 2 * j + g:21 + 2 * j + g])
                ins.then_inc(yssd, 1)

            for j in range(NT):
                act.wait_ge(xb_tr, j + 1)
                S.activation(Xn[:, j, :], ps[:, 0, :], ACT.Copy).then_inc(xn_ok, 1)
                if j >= 2:
                    act.wait_ge(st_pe, j - 1)
                S.activation(Bn[:, j % 2, :, :].rearrange("p g n -> p (g n)"), ps[:, 1, 0:256], ACT.Copy).then_inc(bn_ok, 1)
                for g in range(GROUPS):
                    act.wait_ge(r_pe, 2 * j + g + 1)
                    if j >= 1:
                        act.wait_ge(mm_ok, 2 * (j - 1) + g + 1)
                    for q in range(4):
                        h = 4 * g + q
                        ins = S.activation(Dm[:, g, q, :], ps[:, 2 + g, q * P:(q + 1) * P], ACT.Exp, bias=nacum[:, j, h:h + 1])
                    ins.then_inc(dm_ok, 1)
                if j >= 1:
                    finish_y(j - 1)
            finish_y(NT - 1)

            for q, f in enumerate((4, 5, 6, 7, 0, 1, 2, 3)):
                act.wait_ge(yT_pe, q + 1)
                if f >= 4:
                    S.activation(actT_hi[:, f, :], ps[:, f, :], ACT.Copy).then_inc(yT_hi, 1)
                else:
                    S.activation(actT_hi[:, f, :], ps[:, f, :], ACT.Copy, scale=vecT[:, 51 + f:52 + f]).then_inc(yT_hi, 1)
            high(11)
            act.wait_ge(bias_in, 64)
            S.activation(biasB[0:64, :], biasR[0:64, :], ACT.Copy).then_inc(bias_hi, 1)
            for j in range(NT):
                act.wait_ge(x2_ok, j + 1)
                if j:
                    act.wait_ge(x2sq, j)
                S.activation(x2junk[:, :], x2[:, j, :], ACT.Square, accum_out=ss[:, 12 + j:13 + j]).then_inc(x2sq, 1)
            act.wait_ge(x2sq, NT)
            for j in range(NT):
                act.wait_ge(h2t_pe, j + 1)
                if j >= 2:
                    act.wait_ge(lg_pe, j - 1)
                S.activation(h2T[:, j % 2, :, :].rearrange("p (a k) n -> p a (k n)", a=2), ps[:, 2 * j:2 * j + 2, :],
                             ACT.Copy).then_inc(h2t_act, 1)
            act.wait_ge(ge_in, 1)
            S.activation(gate[:, :, :], gate[:, :, :], ACT.Exp).then_inc(ge_ok, 1)

            both = lambda t: t[:, :, :].rearrange("p (a k) n -> p a (k n)", a=2)

            def high_x(n0, w0, k):
                act.wait_ge(split_used, n0 + (k - SPL + 1))
                act.wait_ge(raw_in[k % RAW], w0 + 16 * (k // RAW + 1))
                S.activation(whi[:, k % SPL, :], raw[:, k % RAW, :], ACT.Copy).then_inc(hi_done, 1)

            def rows_high(X):
                act.wait_ge(xt_pe, past(X + 1))
                S.activation(both(XT_hi), ps[:, 6:8, :], ACT.Copy).then_inc(xt_hi, 1)

            def hidden_high(E):
                act.wait_ge(ht_pe, E + 1)
                S.activation(both(HT_hi), ps[:, 6:8, :], ACT.Copy).then_inc(ht_hi, 1)

            def select(e, dst, done, used, count):
                act.wait_ge(used, past(count))
                S.activation(dst[:, :], esel[:, bass.ds(e, 1)].to_broadcast([P, P]), ACT.Copy).then_inc(done, 1)

            def sigmoid(E, f):
                act.wait_ge(gc_ok, 2 * E + f + 1)
                S.activation(sg[:, f, :], gc[:, f, :], ACT.Sigmoid, scale=ALPHA).then_inc(sg_ok, 1)

            def weighted(E, e):
                act.wait_ge(y_added, 16 * past(E))
                S.activation(idx_s[:, :], idxT[:, bass.ds(e, 1)], ACT.Copy)
                S.activation(ysb[:, :].rearrange("p (a n) -> p a n", a=2), ps[:, 4:6, :], ACT.Copy,
                             scale=gwT[:, bass.ds(e, 1)]).then_inc(y_ok, 1)

            act.wait_ge(bias_zero, 1)

            def one_pass(r):
                E0, X0, n0, w0 = r * NE, r * (NE + 1), r * PASS, r * (16 * PASS // RAW)
                select(0, sel_gu, selg_ok, gub_pe, E0)
                rows_high(X0)
                for c in range(GUC):
                    high_x(n0, w0, N0 + c)
                    if c == 2:
                        select(1, sel_gu, selg_ok, gub_pe, E0 + 1)
                rows_high(X0 + 1)
                sigmoid(E0, 0)
                sigmoid(E0, 1)
                high_x(n0, w0, N0 + GUC)
                high_x(n0, w0, N0 + GUC + 1)
                hidden_high(E0)
                with act.Fori(1, NE) as e:
                    E, X = E0 + e, X0 + e
                    ne, we = n0 + e * EC, w0 + e * (16 * EC // RAW)
                    for c in range(2, EC + 2):
                        high_x(ne, we, N0 + GUC - EC + c)
                        if c == 3:
                            select(e + 1, sel_gu, selg_ok, gub_pe, E + 1)
                        if c == 5:
                            select(e - 1, sel_dn, seld_ok, dnb_pe, E - 1)
                        if c == 10:
                            rows_high(X + 1)
                            sigmoid(E, 0)
                        if c == 11:
                            sigmoid(E, 1)
                    hidden_high(E)
                    weighted(E - 1, e - 1)
                select(NE - 1, sel_dn, seld_ok, dnb_pe, E0 + (NE - 1))
                high_x(n0, w0, N0 + PASS - 2)
                high_x(n0, w0, N0 + PASS - 1)
                act.wait_ge(split_used, n0 + (N0 + PASS))
                weighted(E0 + (NE - 1), NE - 1)

            act.wait_ge(h2_out, 16 * NT)
            passes(act, one_pass)
            for j in range(NT):
                act.wait_ge(fin_in[j], 16)
                if j:
                    act.wait_ge(fsq_ok, j)
                S.activation(fsq[:, :], fin[:, j, :], ACT.Square, accum_out=ss[:, 16 + j:17 + j]).then_inc(fsq_ok, 1)
            for j in range(NT):
                act.wait_ge(fo_ok, j + 1)
                act.dma_start(out[0, j * P:(j + 1) * P, :], fin[:, j, :]).then_inc(out_done, 16)
            act.wait_ge(out_done, 16 * NT)

        @block.vector
        def _(dve):
            Vv = nc.vector
            link = Chain(dve, dve_own)

            def low(n):
                dve.wait_ge(hi_done, n + 1)
                w = block_of(n)[1]
                Vv.tensor_tensor(wlo[:, n % SPL, 0:w], raw[:, n % RAW, 0:w], whi[:, n % SPL, 0:w], ALU.subtract).then_inc(lo_dve, 1)

            for j in range(NT):
                dve.wait_ge(x_rms, j + 1)
                Vv.tensor_scalar(xnat[:, j, :], xnat[:, j, :], rstd[:, j:j + 1], None, ALU.mult).then_inc(xs_ok, 1)
            for n in range(3):
                low(n)
            for k in range(KD):
                dve.wait_ge(hT_hi_ok, k + 1)
                Vv.scalar_tensor_tensor(out=actT_lo[:, k, :], in0=ps[:, k, :], scalar=vecT[:, k:k + 1],
                                        in1=actT_hi[:, k, :], op0=ALU.mult, op1=ALU.subtract).then_inc(hT_lo_ok, 1)
            dve.wait_ge(pos_in, 32)
            link(Vv.tensor_copy(posf[:, :], posi[:, :]))
            link(Vv.tensor_scalar(posf[:, :], posf[:, :], frq[:, 0:1], None, ALU.mult))
            for dst, shift in ((ang, 0.25), (angk, 0.0)):
                turns = acc2[:, 0, :]
                link(Vv.tensor_scalar(turns, posf[:, :], 1.0 / TWO_PI, shift, ALU.mult, ALU.add))
                link(Vv.tensor_scalar(turns, turns, MAGIC, None, ALU.add))
                link(Vv.tensor_scalar(turns, turns, MAGIC, None, ALU.subtract))
                link(Vv.scalar_tensor_tensor(out=dst[:, :], in0=turns, scalar=-C1, in1=posf[:, :], op0=ALU.mult, op1=ALU.add))
                link(Vv.scalar_tensor_tensor(out=dst[:, :], in0=turns, scalar=-C2, in1=dst[:, :], op0=ALU.mult, op1=ALU.add))
                link(Vv.scalar_tensor_tensor(out=dst[:, :], in0=turns, scalar=-C3, in1=dst[:, :], op0=ALU.mult, op1=ALU.add))
                if shift:
                    link(Vv.tensor_scalar(dst[:, :], dst[:, :], shift * TWO_PI, None, ALU.add))
                Vv.tensor_scalar(dst[:, :], dst[:, :], 3.141592, -3.141592, ALU.min, ALU.max).then_inc(trig_in, 1)
            low(3)
            low(4)
            dve.wait_ge(lat_sq, 2 * NT)
            dve.wait_ge(par_in, 48)
            Vv.tensor_tensor(dt[:, :, :], ps[:, 0:4, 0:8], dtb[:, :].unsqueeze(1).to_broadcast([P, NT, HEADS]), ALU.add).then_inc(dt_in, 1)
            kr0 = 8 + QR + KVR
            Vv.tensor_copy(krn[:, :, 0, :], ps[:, 0:4, kr0:kr0 + ROPE])
            Vv.tensor_copy(krn[:, :, 1, 0:ROPE // 2], ps[:, 0:4, kr0 + ROPE // 2:kr0 + ROPE])
            Vv.tensor_copy(krn[:, :, 1, ROPE // 2:ROPE], ps[:, 0:4, kr0:kr0 + ROPE // 2])
            dve.wait_ge(lat_rms, 2)
            for j in range(NT):
                Vv.tensor_scalar(latn[:, j, 0:QR], ps[:, j, 8:8 + QR], rstd[:, 4 + j:5 + j], None, ALU.mult)
                Vv.tensor_scalar(latn[:, j, QR:QR + KVR], ps[:, j, 8 + QR:kr0], rstd[:, 8 + j:9 + j], None, ALU.mult).then_inc(lat_ok, 1)
            dve.wait_ge(dt_e, 3)
            link(Vv.scalar_tensor_tensor(out=dt[:, :, :], in0=dt[:, :, :], scalar=0.0, in1=dtx[:, :, :], op0=ALU.max, op1=ALU.add))
            Vv.scalar_tensor_tensor(out=adt[:, :, :], in0=dt[:, :, :], scalar=-1.0,
                                    in1=alog[:, :].unsqueeze(1).to_broadcast([P, NT, HEADS]),
                                    op0=ALU.mult, op1=ALU.mult).then_inc(adt_ok, 1)
            low(5)

            def conv(m):
                dve.wait_ge(u_ok, m + 1)
                if m >= 2:
                    dve.wait_ge(xbc_ok, m - 1)
                a, u = acc2[:, m % 2, :], U[:, m % 4, :]
                tap = lambda q: vecT[:, 8 + 8 * q + m:9 + 8 * q + m]
                link(Vv.tensor_scalar(a, u[:, 0:SEQ], tap(0), None, ALU.mult))
                for q in range(1, 4):
                    ins = Vv.scalar_tensor_tensor(out=a, in0=u[:, q:q + SEQ], scalar=tap(q), in1=a, op0=ALU.mult, op1=ALU.add)
                    if q < 3:
                        link(ins)
                ins.then_inc(conv_ok, 1)

            dve.wait_ge(pad_ok, 1)
            for m in range(4):
                conv(m)
                if m == 1:
                    low(6)
            low(7)
            for m in range(4, 8):
                conv(m)
                if m == 5:
                    low(8)
            low(9)
            low(10)

            dve.wait_ge(trig_ok, 1)
            for i, (kind, a, eng) in enumerate(MLA):
                if eng != "D":
                    continue
                b = i % 8
                dve.wait_ge(mla_pe, i + 1)
                if kind == "lat":
                    Vv.tensor_scalar(cqT[:, a, :], ps[:, b, :], vecT[:, 48 + a:49 + a], None, ALU.mult).then_inc(mla_dve, 1)
                elif kind == "kr":
                    dst, tab = ((ropeS, COS), (ropeR, SIN))[a]
                    Vv.tensor_tensor(dst[0:ROPE, :], ps[0:ROPE, b, :], tab[0:ROPE, :], ALU.mult).then_inc(mla_dve, 1)
                    if a == 1:
                        mla_evacuated(dve, i)
                        Vv.tensor_tensor(krf[:, :], ropeS[0:ROPE, :], ropeR[0:ROPE, :], ALU.add).then_inc(kr_sum, 1)
                        dve.wait_ge(kr_sum, 1)
                        for h in range(4):
                            ins = Vv.tensor_copy(KT[NOPE:QK, h, :], krf[:, :])
                        ins.then_inc(kr_dve, 1)
                elif kind in ("qn", "kn"):
                    dst = QT if kind == "qn" else KT
                    Vv.tensor_copy(dst[0:NOPE, 2 * a, :], ps[0:NOPE, b, :])
                    Vv.tensor_copy(dst[0:NOPE, 2 * a + 1, :], ps[NOPE:P, b, :]).then_inc(mla_dve, 1)
                elif kind == "qs":
                    mla_evacuated(dve, i - 1)
                    dve.wait_ge(kr_dve, 1)
                    Vv.tensor_tensor(ropeS[:, :], ps[:, b, :], COS[:, :], ALU.mult).then_inc(mla_dve, 1)
                elif kind == "qr":
                    link(Vv.tensor_tensor(ropeR[:, :], ps[:, b, :], SIN[:, :], ALU.mult))
                    for q in range(4):
                        rows = slice(q * ROPE, (q + 1) * ROPE)
                        ins = Vv.tensor_tensor(QT[NOPE:QK, 4 * a + q, :], ropeS[rows, :], ropeR[rows, :], ALU.add)
                    ins.then_inc(mla_dve, 1)
                else:
                    Vv.tensor_copy(V[:, a, :], ps[:, b, :]).then_inc(mla_dve, 1)

            def pt_copy(u):
                dve.wait_ge(pt_done, u + 1)
                if u >= 2:
                    dve.wait_ge(pv_done, u - 1)
                n = u // HEADS + 1
                Vv.tensor_copy(PT[:, u % 2, 0:n, :].rearrange("p k n -> p (k n)"), ps[:, 2 + u % 2, 0:n * P]).then_inc(pt_dve, 1)

            def attended(i):
                dve.wait_ge(pv_done, HEADS * (i + 1))
                link(Vv.reciprocal(rsum[:, 8 * i:8 * i + 8], rsum[:, 8 * i:8 * i + 8]))
                Vv.tensor_tensor(Ynat[:, i, SSDW:DM].rearrange("p (h d) -> p h d", h=HEADS),
                                 ps[:, 4 + i % 2, :].rearrange("p (h d) -> p h d", h=HEADS),
                                 heads(rsum[:, 8 * i:8 * i + 8], VD), ALU.mult).then_inc(ymla, 1)

            for u in range(NU):
                dve.wait_ge(s_done, u + 1)
                link(Vv.reduce_max(mraw[:, u:u + 1], ps[:, u % 2, 0:(u // HEADS + 1) * P], AX))
                Vv.tensor_scalar(nmax[:, u:u + 1], mraw[:, u:u + 1], -SCALE, None, ALU.mult).then_inc(nm_done, 1)
                if u % 2 == 1:
                    pt_copy(u - 1)
                if u % HEADS == 3 and u > HEADS:
                    attended(u // HEADS - 1)
            attended(NT - 1)

            fl = lambda t: t[:, :, :].rearrange("p j h -> p (j h)")
            dve.wait_ge(cum_pe, 1)
            Vv.tensor_scalar(fl(nacum), ps[:, 7, 0:32], -1.0, None, ALU.mult).then_inc(cum_dve, 1)
            dve.wait_ge(cum_dve, 1)
            Vv.tensor_tensor(fl(dtx), ps[:, 7, 32:64], fl(nacum), ALU.add).then_inc(cum_dve, 1)
            dve.wait_ge(cum_act, 3)
            by_head = lambda t: t.rearrange("p (h d) -> p h d", h=HEADS)
            for j in range(NT):
                dve.wait_ge(bn_ok, j + 1)
                if j >= 1:
                    dve.wait_ge(yd_pe, j)
                for g in range(GROUPS):
                    dve.wait_ge(dm_ok, 2 * j + g + 1)
                    Vv.tensor_tensor(Mm[:, g, :, :], Dm[:, g, :, :],
                                     ps[:, 1, (2 + g) * P:(3 + g) * P].unsqueeze(1).to_broadcast([P, 4, P]),
                                     ALU.mult).then_inc(mm_ok, 1)
                if j < NT - 1:
                    dve.wait_ge(st_pe, j + 1)
                    if j == 0:
                        Vv.tensor_copy(hst[:, :], ps[:, 7, :]).then_inc(h_ok, 1)
                    else:
                        dve.wait_ge(hm_ok, j)
                        dve.wait_ge(yo_pe, j)
                        Vv.tensor_tensor(hst[:, :], htmp[:, :], ps[:, 7, :], ALU.add).then_inc(h_ok, 1)
                dve.wait_ge(yd_pe, j + 1)
                if j == 0:
                    Vv.tensor_copy(yt[:, :], ps[:, 4, :]).then_inc(y1_ok, 1)
                else:
                    dve.wait_ge(y2_ok, j)
                    dve.wait_ge(yo_pe, j)
                    link(Vv.tensor_tensor(by_head(yt[:, :]), by_head(ps[:, 6, :]), heads(eacum[:, j, :], HD), ALU.mult))
                    Vv.tensor_tensor(yt[:, :], yt[:, :], ps[:, 4 + j % 2, :], ALU.add).then_inc(y1_ok, 1)

            for q, f in enumerate((4, 5, 6, 7, 0, 1, 2, 3)):
                dve.wait_ge(yT_hi, q + 1)
                if f >= 4:
                    Vv.tensor_tensor(actT_lo[:, f, :], ps[:, f, :], actT_hi[:, f, :], ALU.subtract).then_inc(yT_lo, 1)
                else:
                    Vv.scalar_tensor_tensor(out=actT_lo[:, f, :], in0=ps[:, f, :], scalar=vecT[:, 51 + f:52 + f],
                                            in1=actT_hi[:, f, :], op0=ALU.mult, op1=ALU.subtract).then_inc(yT_lo, 1)
            low(11)
            dve.wait_ge(bias_hi, 1)
            dve.wait_ge(bias_zero, 1)
            Vv.tensor_tensor(biasB[32:64, :], biasR[32:64, :], biasB[32:64, :], ALU.subtract).then_inc(bias_lo, 1)
            dve.wait_ge(split_used, N0)
            dve.wait_ge(xr_in, 64)
            for j in range(NT):
                Vv.tensor_tensor(x2[:, j, :].rearrange("p (a n) -> p a n", a=2), ps[:, 2 * j:2 * j + 2, :],
                                 x2[:, j, :].rearrange("p (a n) -> p a n", a=2), ALU.add).then_inc(x2_ok, 1)
            dve.wait_ge(gn_in, 32)
            for j in range(NT):
                dve.wait_ge(x2_rms, j + 1)
                Vv.scalar_tensor_tensor(out=h2[:, j, :], in0=x2[:, j, :], scalar=rstd[:, 12 + j:13 + j], in1=gffn[:, :],
                                        op0=ALU.mult, op1=ALU.mult).then_inc(h2_ok, 1)
            for j in range(NT):
                dve.wait_ge(lg_pe, j + 1)
                link(Vv.tensor_tensor(lgt[:, j, :], ps[:, 2 * j, 0:NE], brt[:, :], ALU.add))
                link(Vv.max(top8[:, j, :], lgt[:, j, :]))
                link(Vv.max_index(topi[:, j, :], top8[:, j, :], lgt[:, j, :]))
            Vv.tensor_tensor(gate[:, :, :], top8[:, :, 0:TOPK], top8[:, :, 0:1].to_broadcast([P, NT, TOPK]), ALU.subtract).then_inc(ge_in, 1)
            link(Vv.tensor_copy(topf[:, :, :], topi[:, :, 0:TOPK]))
            pairs = lambda t: t[:, :, :].rearrange("p j k -> p (j k)").unsqueeze(2).to_broadcast([P, NT * TOPK, NE])
            over_k = lambda t: t[:, :, :].rearrange("p (j k) e -> p j e k", k=TOPK)
            dve.wait_ge(iota_ok, 2)
            link(Vv.tensor_tensor(eq[:, :, :], iota_f[:, 0:NE].unsqueeze(1).to_broadcast([P, NT * TOPK, NE]), pairs(topf), ALU.is_equal))
            Vv.tensor_reduce(mask[:, :, :], over_k(eq), AX, ALU.add).then_inc(mask_ok, 1)
            dve.wait_ge(ge_ok, 1)
            link(Vv.tensor_reduce(gsum[:, :], gate[:, :, :], AX, ALU.add))
            link(Vv.reciprocal(gsum[:, :], gsum[:, :]))
            link(Vv.tensor_tensor(gate[:, :, :], gate[:, :, :], gsum[:, :].unsqueeze(2).to_broadcast([P, NT, TOPK]), ALU.mult))
            link(Vv.tensor_tensor(eqg[:, :, :], eq[:, :, :], pairs(gate), ALU.mult))
            dve.wait_ge(tg_ok, 2)
            Vv.tensor_reduce(TG[:, :, 0:NE, 1], over_k(eqg), AX, ALU.add)
            dve.wait_ge(rank_pe, 1)
            dve.wait_ge(mask_ok, 1)
            dve.wait_ge(iota_ok, 2)
            link(Vv.scalar_tensor_tensor(out=rank[:, :, 0:NE], in0=ps[:, 1, 0:NT * NE].rearrange("p (j e) -> p j e", j=NT),
                                         scalar=1.0, in1=mask[:, :, :], op0=ALU.add, op1=ALU.mult))
            link(Vv.tensor_scalar(rank[:, :, 0:NE], rank[:, :, 0:NE], -1.0, None, ALU.add))
            link(Vv.reduce_max(cntf[:, 0:1], ps[:, 3, 0:NE], AX))
            Vv.tensor_copy(cnti[:, 0:1], cntf[:, 0:1]).then_inc(route_ok, 1)

            both = lambda t: t[:, :, :].rearrange("p (a k) n -> p a (k n)", a=2)

            def low_x(n0, k):
                dve.wait_ge(hi_done, n0 + (k + 1))
                Vv.tensor_tensor(wlo[:, k % SPL, 0:DVE_COLS], raw[:, k % RAW, 0:DVE_COLS], whi[:, k % SPL, 0:DVE_COLS],
                                 ALU.subtract).then_inc(lo_dve, 1)

            def places(D, e):
                dve.wait_ge(disp_pe, past(D))
                Vv.tensor_tensor(onehot[:, :, :], iota_f[:, :].unsqueeze(1).to_broadcast([P, NT, P]),
                                 rank[:, :, bass.ds(e, 1)].to_broadcast([P, NT, P]), ALU.is_equal).then_inc(oh_ok, 1)

            def table(D, e, first=False):
                dve.wait_ge(disp_pe, past(D + 1))
                if not first:
                    dve.wait_ge(x_got, 16 * D)
                Vv.tensor_copy(gwT[:, bass.ds(e, 1)], ps[:, 6, 1:2])
                Vv.tensor_copy(idx_f[:, :], ps[:, 6, 0:1]).then_inc(disp_t, 1)
                dve.wait_ge(disp_t, 2 * D + 1)
                Vv.scalar_tensor_tensor(out=idx_f[:, :], in0=ps[:, 6, 2:3], scalar=smid[:, 0:1], in1=idx_f[:, :],
                                        op0=ALU.mult, op1=ALU.add).then_inc(disp_t, 1)
                dve.wait_ge(disp_t, 2 * D + 2)
                Vv.tensor_scalar(idxT[:, bass.ds(e, 1)], idx_f[:, :], smid[:, 1:2], None, ALU.add)
                Vv.tensor_scalar(idx_g[:, :], idx_f[:, :], smid[:, 1:2], None, ALU.add).then_inc(idx_ok, 1)

            def rows_low(X):
                dve.wait_ge(xt_hi, X + 1)
                Vv.tensor_tensor(both(XT_lo), ps[:, 6:8, :], both(XT_hi), ALU.subtract).then_inc(xt_lo, 1)

            def hidden_low(E):
                dve.wait_ge(ht_hi, past(E + 1))
                Vv.tensor_tensor(both(HT_lo), ps[:, 6:8, :], both(HT_hi), ALU.subtract).then_inc(ht_lo, 1)

            def clamp(E, done):
                dve.wait_ge(split_used, done)
                for f in range(2):
                    Vv.tensor_scalar(gc[:, f, :], ps[:, f, :], LIMIT, None, ALU.min).then_inc(gc_ok, 1)
                    Vv.tensor_scalar(uc[:, f, :], ps[:, 2 + f, :], LIMIT, -LIMIT, ALU.min, ALU.max).then_inc(uc_ok, 1)

            def hidden(E):
                dve.wait_ge(uc_ok, past(2 * E + 2))
                dve.wait_ge(gc_ok, 2 * E + 2)
                for f in range(2):
                    Vv.scalar_tensor_tensor(out=uc[:, f, :], in0=uc[:, f, :], scalar=1.0, in1=gc[:, f, :],
                                            op0=ALU.add, op1=ALU.mult).then_inc(t_ok, 1)
                dve.wait_ge(t_ok, 2 * E + 2)
                for f in range(2):
                    dve.wait_ge(sg_ok, 2 * E + (f + 1))
                    Vv.tensor_tensor(uc[:, f, :], uc[:, f, :], sg[:, f, :], ALU.mult).then_inc(h_act, 1)

            def one_pass(r):
                E0, X0, D0, n0 = r * NE, r * (NE + 1), r * PADE, r * PASS
                dve.wait_ge(rank_ok, past(r))
                places(D0, 0)
                table(D0, 0, first=True)
                places(D0 + 1, 1)
                rows_low(X0)
                table(D0 + 1, 1)
                for c in range(GUC):
                    low_x(n0, N0 + c)
                    if c == 2:
                        places(D0 + 2, 2)
                    if c == 5:
                        table(D0 + 2, 2)
                rows_low(X0 + 1)
                clamp(E0, n0 + (N0 + GUC))
                hidden(E0)
                low_x(n0, N0 + GUC)
                low_x(n0, N0 + GUC + 1)
                hidden_low(E0)
                with dve.Fori(1, NE) as e:
                    E, X, D, ne = E0 + e, X0 + e, D0 + e, n0 + e * EC
                    for c in range(2, EC + 2):
                        low_x(ne, N0 + GUC - EC + c)
                        if c == 2:
                            places(D + 2, e + 2)
                        if c == 5:
                            table(D + 2, e + 2)
                        if c == 10:
                            rows_low(X + 1)
                            clamp(E, ne + (N0 + 2 * GUC - EC))
                        if c == 11:
                            hidden(E)
                    hidden_low(E)
                low_x(n0, N0 + PASS - 2)
                low_x(n0, N0 + PASS - 1)
                dve.wait_ge(oh_ok, D0 + PADE)
                dve.wait_ge(x_got, 16 * (D0 + PADE))
                Vv.tensor_scalar(rank[:, :, :], rank[:, :, :], -float(P), None, ALU.add).then_inc(rank_ok, 1)

            dve.wait_ge(h2_out, 16 * NT)
            passes(dve, one_pass)
            for j in range(NT):
                dve.wait_ge(f_rms, j + 1)
                Vv.scalar_tensor_tensor(out=fin[:, j, :], in0=fin[:, j, :], scalar=rstd[:, 16 + j:17 + j], in1=gfin[:, :],
                                        op0=ALU.mult, op1=ALU.mult).then_inc(fo_ok, 1)

        @block.gpsimd
        def _(pool):
            G = nc.gpsimd
            link = Chain(pool, pool_own)

            def keep(t, cmp, fill, base, step, per_row, cols=P):
                return G.affine_select(out=t, in_=t, compare_op=cmp, fill=fill, base=base, pattern=[[step, cols]],
                                       channel_multiplier=per_row)

            for s in (gub_pe, dnb_pe, disp_pe, xt_pe, ht_hi, ht_lo, uc_ok, y_ok, rank_ok):
                pool.sem_inc(s, past(0))
            G.memset(Uinc[:, :], 1.0)
            G.memset(onesf[:, :], 1.0)
            G.memset(mhalf[:, :], -0.5)
            G.memset(identb[:, :], 0.0)
            G.memset(maskA[:, :], 0.0)
            G.memset(maskS[:, :], 0.0)
            G.memset(esel[:, :], 0.0)
            link(G.memset(ident[:, :], 0.0))
            keep(ident[:, :], ALU.not_equal, 1.0, 0, -1, 1).then_inc(konst_ok, 1)
            keep(Uinc[:, :], ALU.is_ge, 0.0, 0, 1, -1)
            keep(identb[:, :], ALU.not_equal, 1.0, 0, -1, 1)
            keep(maskA[:, :], ALU.is_ge, NEG, 0, -1, 1)
            keep(maskS[:, :], ALU.is_ge, NEG, 0, 1, -1)
            link(keep(esel[:, :], ALU.not_equal, 1.0, 0, -1, 1, PADE))
            link(keep(esel[:, :], ALU.not_equal, 1.0, -32, -1, 1, PADE))
            link(G.iota(kint[:, :], pattern=[[1, P]], base=0, channel_multiplier=0))
            link(G.tensor_copy(iota_f[:, :], kint[:, :]))
            link(G.iota(kint[:, 0:1], pattern=[[1, 1]], base=0, channel_multiplier=1))
            link(G.tensor_copy(smid[:, 3:4], kint[:, 0:1]))
            G.tensor_scalar(smid[:, 0:1], smid[:, 3:4], -1.0, 0.0, ALU.mult, ALU.add)
            G.tensor_scalar(smid[:, 1:2], smid[:, 3:4], 1.0, float(TRASH), ALU.mult, ALU.add)
            G.tensor_scalar(smid[:, 2:3], smid[:, 3:4], 1.0, -float(SEQ), ALU.mult, ALU.add).then_inc(iota_ok, 2)
            G.memset(U[:, :, 0:3], 0.0).then_inc(pad_ok, 1)

            def low(n):
                pool.wait_ge(hi_done, n + 1)
                w, d = block_of(n)
                G.tensor_tensor(wlo[:, n % SPL, d:w], raw[:, n % RAW, d:w], whi[:, n % SPL, d:w], ALU.subtract).then_inc(lo_pool, 1)

            def inv_rms(c, n, width):
                link(G.tensor_scalar(rstd[:, c:c + n], ss[:, c:c + n], 1.0 / width, EPS, ALU.mult, ALU.add))
                return G.tensor_tensor(rstd[:, c:c + n], rstd[:, c:c + n], mhalf[:, 0:n], ALU.pow)

            for j in range(NT):
                pool.wait_ge(xsq, j + 1)
                inv_rms(j, 1, DM).then_inc(x_rms, 1)
            for n in range(5):
                low(n)
            pool.wait_ge(lat_sq, 2 * NT)
            inv_rms(4, 4, QR).then_inc(lat_rms, 1)
            inv_rms(8, 4, KVR).then_inc(lat_rms, 1)
            for n in range(5, 11):
                low(n)

            by_head = lambda t: t.rearrange("p (h d) -> p h d", h=HEADS)

            def gated(j):
                pool.wait_ge(y1_ok, j + 1)
                link(G.tensor_tensor(by_head(ydx[:, :]), by_head(Xn[:, j, :]), heads(dsk[:, :], HD), ALU.mult))
                link(G.tensor_tensor(ydx[:, :], ydx[:, :], yt[:, :], ALU.add))
                G.tensor_tensor(Ynat[:, j, 0:SSDW], ydx[:, :], sz[:, j, :], ALU.mult).then_inc(y2_ok, 1)
                pool.wait_ge(ysq, 2 * j + 2)
                inv_rms(20 + 2 * j, 2, 256).then_inc(y_rms, 1)

            pool.wait_ge(par_in, 48)
            pool.wait_ge(sz_ok, NT)
            for j in range(NT):
                pool.wait_ge(xn_ok, j + 1)
                if j == 0:
                    pool.wait_ge(cum_act, 3)
                if j >= 2:
                    pool.wait_ge(yd_pe, j - 1)
                    pool.wait_ge(st_pe, j - 1)
                G.tensor_tensor(by_head(xd[:, j % 2, :]), by_head(Xn[:, j, :]), heads(dt[:, j, :], HD), ALU.mult).then_inc(xd_ok, 1)
                if j < NT - 1:
                    pool.wait_ge(xd_ok, j + 1)
                    G.tensor_tensor(by_head(xdd[:, j % 2, :]), by_head(xd[:, j % 2, :]), heads(dte[:, j, :], HD), ALU.mult).then_inc(xdd_ok, 1)
                    if j >= 1:
                        pool.wait_ge(h_ok, j)
                        G.tensor_tensor(by_head(htmp[:, :]), by_head(hst[:, :]), heads(cdec[:, j, :], HD), ALU.mult).then_inc(hm_ok, 1)
                if j >= 1:
                    gated(j - 1)
            gated(NT - 1)

            pool.wait_ge(yssd, NT)
            for j in range(NT):
                pool.dma_start(x2[:, j, :], A["x"][0, j * P:(j + 1) * P, :]).then_inc(xr_in, 16)
            pool.dma_start(gffn[:, :], A["norm_ffn_g"][0].partition_broadcast(P)).then_inc(gn_in, 16)
            pool.dma_start(gfin[:, :], A["norm_final_g"].partition_broadcast(P)).then_inc(gn_in, 16)
            for q in range(2):
                rows = slice(32 * q, 32 * q + NE)
                pool.dma_start(biasR[rows, 0:2 * DFF], A["b_gate_up"][0]).then_inc(bias_in, 16)
                pool.dma_start(biasR[rows, 2 * DFF:3 * DFF], A["b_down"][0]).then_inc(bias_in, 16)
            G.memset(biasB[64:P, :].bitcast(F32), 0.0).then_inc(bias_zero, 1)
            pool.wait_ge(bias_zero, 1)
            link(G.memset(Ustrict[:, :], 1.0))
            keep(Ustrict[:, :], ALU.is_gt, 0.0, 0, 1, -1).then_inc(tg_ok, 1)
            G.memset(rank[:, :, NE:PADE], -1.0)
            link(G.memset(TG[:, :, :, :], 0.0))
            pool.wait_ge(iota_ok, 2)
            G.tensor_scalar(TG[:, :, :, 2], TG[:, :, :, 2], 1.0, 1.0, ALU.mult, ALU.add)
            for j in range(NT):
                ins = G.tensor_scalar(TG[:, j, :, 0], TG[:, j, :, 0], smid[:, 2:3], float(j * P), ALU.add, ALU.add)
            ins.then_inc(tg_ok, 1)
            low(11)
            pool.wait_ge(split_used, N0)
            link(G.memset(Xg[:, :], 0.0))
            pool.dma_start(acc_d[SEQ:SEQ + P, :], Xg[:, :]).then_inc(y_added, 16 * past(0))
            for j in range(NT):
                pool.wait_ge(x2_ok, j + 1)
                pool.dma_start(acc_d[j * P:(j + 1) * P, :], x2[:, j, :]).then_inc(acc_out, 16)
            for j in range(NT):
                pool.wait_ge(x2sq, j + 1)
                inv_rms(12 + j, 1, DM).then_inc(x2_rms, 1)
            for j in range(NT):
                pool.wait_ge(h2_ok, j + 1)
                pool.dma_start(h2_d[j * P:(j + 1) * P, :], h2[:, j, :]).then_inc(h2_out, 16)
            pool.wait_ge(y_added, 16 * past(0))
            pool.wait_ge(acc_out, 16 * NT)
            pool.wait_ge(h2_out, 16 * NT)

            def low_x(n0, k):
                pool.wait_ge(hi_done, n0 + (k + 1))
                G.tensor_tensor(wlo[:, k % SPL, DVE_COLS:], raw[:, k % RAW, DVE_COLS:], whi[:, k % SPL, DVE_COLS:],
                                ALU.subtract).then_inc(lo_pool, 1)

            def gather(D, X):
                pool.wait_ge(idx_ok, D + 1)
                pool.wait_ge(xt_pe, past(X))
                pool.sem_inc(rows_asked, 1)
                G.indirect_dma_start(Xg[:, :], None, h2_d, bass.IndirectOffsetOnAxis(idx_g[:, 0:1], 0),
                                     bounds_check=SEQ - 1, oob_is_err=False).then_inc(x_got, 16)

            def scatter(E, e):
                pool.wait_ge(y_ok, past(E + 1))
                pool.sem_inc(rows_sent, 1)
                G.indirect_dma_start(acc_d, bass.IndirectOffsetOnAxis(idx_s[:, 0:1], 0), ysb[:, :], None,
                                     compute_op=ALU.add).then_inc(y_added, 16)

            def one_pass(r):
                E0, X0, D0, n0 = r * NE, r * (NE + 1), r * PADE, r * PASS
                gather(D0, X0)
                gather(D0 + 1, X0 + 1)
                for c in range(GUC + 2):
                    low_x(n0, N0 + c)
                gather(D0 + 2, X0 + 2)
                with pool.Fori(1, NE) as e:
                    E, X, D, ne = E0 + e, X0 + e, D0 + e, n0 + e * EC
                    for c in range(2, EC + 2):
                        low_x(ne, N0 + GUC - EC + c)
                        if c == 11:
                            gather(D + 2, X + 2)
                    scatter(E - 1, e - 1)
                low_x(n0, N0 + PASS - 2)
                low_x(n0, N0 + PASS - 1)
                scatter(E0 + (NE - 1), NE - 1)
                pool.wait_ge(y_added, 16 * past(E0 + NE))

            passes(pool, one_pass)
            for j in range(NT):
                pool.dma_start(fin[:, j, :], acc_d[j * P:(j + 1) * P, :]).then_inc(fin_in[j], 16)
            for j in range(NT):
                pool.wait_ge(fsq_ok, j + 1)
                inv_rms(16 + j, 1, DM).then_inc(f_rms, 1)


_INS = ['x', 'positions', 'norm_mix_g', 'w_in', 'conv_w', 'conv_b', 'dt_bias', 'a_log', 'd_skip', 'ssd_norm_g',
        'q_norm_g', 'w_uq', 'kv_norm_g', 'w_ukv', 'w_out', 'norm_ffn_g', 'w_router', 'b_router',
        'w_gate_up', 'b_gate_up', 'w_down', 'b_down', 'norm_final_g']


def kernel(**inputs):
    import concourse.bacc as bacc
    from concourse.bass_utils import run_bass_kernel_spmd

    nc = bacc.Bacc("TRN2", target_bir_lowering=False, num_devices=1)
    half = np.arange(P) % (ROPE // 2)
    freq = np.power(np.float32(10000.0), -(2 * half).astype(np.float32) / np.float32(ROPE)).astype(np.float32)
    sign = np.where(np.arange(P) % ROPE < ROPE // 2, -1.0, 1.0).astype(np.float32)
    arrays, args = {}, {}
    for name in _INS + ['rope_freq']:
        a = np.stack([freq, sign], axis=1) if name == 'rope_freq' else np.ascontiguousarray(inputs[name])
        arrays[f"in_{name}_dram"] = a
        args[name] = nc.dram_tensor(f"in_{name}_dram", a.shape, mybir.dt.from_np(a.dtype), kind="ExternalInput").ap()
    out = nc.dram_tensor("out_0_dram", (1, SEQ, DM), F32, kind="ExternalOutput").ap()
    layer(nc, args, out)
    r = run_bass_kernel_spmd(nc, [arrays], core_ids=[0])
    return r.results[0]["out_0_dram"]
```

```python
from contextlib import ExitStack

import numpy as np
import concourse.bass as bass
from concourse import mybir

F32 = mybir.dt.float32
F32R = mybir.dt.float32r
BF16 = mybir.dt.bfloat16
I32 = mybir.dt.int32
U32 = mybir.dt.uint32
ALU = mybir.AluOpType
ACT = mybir.ActivationFunctionType
AX = mybir.AxisListType.X

P = 128
SEQ, DM = 512, 1024
NT = SEQ // P
KD = DM // P
EPS = 1e-6
HEADS, HD, STATE, GROUPS = 8, 64, 128, 2
SSDW = HEADS * HD
QR, KVR, NOPE, ROPE, VD = 256, 128, 64, 32, 64
QK = NOPE + ROPE
SCALE = QK ** -0.5
NE, TOPK, DFF = 32, 4, 1024
LIMIT, ALPHA = 7.0, 1.702
NEG = -1e30
CHUNK = 2048
RAW, SPL = 4, 3
XRAW = 6
DVE_COLS = 1664
IN_CHUNKS, OUT_CHUNKS = 8, 4
OUT_ORDER = (4, 5, 6, 7, 0, 1, 2, 3)
N0 = IN_CHUNKS + OUT_CHUNKS
GUC, DNC = 8, 4
EC = GUC + DNC
PASS = NE * EC
SMALL = 424
PADE = NE + 2
TRASH = SEQ
TWO_PI = 6.283185307179586
C1 = 6.28125
C2 = float(np.float32(0.0019353071795864769))
C3 = float(TWO_PI - C1 - C2)
MAGIC = 12582912.0


def block_of(n):
    return (4 * SMALL, 1408) if n < 2 else (CHUNK, DVE_COLS)


MLA = [("lat", 0, "A"), ("lat", 1, "D"), ("lat", 2, "A"), ("kr", 0, "D"), ("kr", 1, "D"),
       ("qn", 0, "A"), ("qn", 1, "D"), ("qn", 2, "A"), ("qn", 3, "D"),
       ("qs", 0, "D"), ("qr", 0, "D"), ("qs", 1, "D"), ("qr", 1, "D"),
       ("kn", 0, "A"), ("kn", 1, "A"), ("kn", 2, "D"), ("kn", 3, "A"),
       ("v", 0, "A"), ("v", 1, "D"), ("v", 2, "A"), ("v", 3, "A")]
WQ = 10
NU = NT * HEADS
S_BANK = (6, 7, 0, 1)


def slot_of(f):
    return 2 * (f - 4) if f >= 4 else 2 * f + 1


def layer(nc, A, out):
    with ExitStack() as ctx:
        base = nc.sbuf_base
        base = (base + 63) // 64 * 64

        def at(name, off, shape, dt=F32):
            return nc.alloc_sbuf_tensor_at(name, shape, dt, offset=base + off)

        def sem(name):
            return ctx.enter_context(nc.semaphore(name))

        raw = at("raw", 0, [P, RAW, CHUNK])
        whi = at("whi", 32768, [P, SPL, CHUNK], F32R)
        wlo = at("wlo", 57344, [P, SPL, CHUNK], F32R)
        RA, RF, RC, RD, RE, RG, RH, RI, RJ, RK = (81920, 114688, 131072, 147456, 155904, 164096,
                                                  172288, 190720, 194816, 198912)
        actT_hi = at("actT_hi", RA, [P, KD, SEQ], F32R)
        actT_lo = at("actT_lo", RA + 16384, [P, KD, SEQ], F32R)
        QT = at("QT", RA, [P, HEADS, SEQ])
        KT = at("KT", RA + 16384, [P, HEADS, SEQ])
        xnat = at("xnat", RF, [P, NT, DM])
        latn = at("latn", RF, [P, NT, QR + KVR])
        krn = at("krn", RF + 6144, [P, NT, 2, ROPE])
        Ynat = at("Ynat", RF, [P, NT, SSDW])
        h2 = at("h2", RF, [P, NT, DM])
        XBC = at("XBC", RC, [P, 8, SEQ])
        x2 = at("x2", RC, [P, NT, DM])
        raw_more = at("raw_more", RC, [P, XRAW - RAW, CHUNK])
        U = at("U", RD, [P, 4, 3 + SEQ])
        Pr = at("Pr", RD, [P, 4, SEQ])
        Dm = at("Dm", RD, [P, GROUPS, 4, P])
        Mm = at("Mm", RD + 4096, [P, GROUPS, 4, P])
        h2T = at("h2T", RA, [P, NT, KD, P])
        sz = at("sz", RE, [P, NT, SSDW])
        V = at("V", RG, [P, NT, SSDW])
        Xn = at("Xn", RG, [P, NT, SSDW])
        wqn = at("wqn", RH, [P, 2, HEADS * NOPE])
        wqs = at("wqs", RH + 4096, [P, 2, HEADS * ROPE])
        wqr = at("wqr", RH + 6144, [P, 2, HEADS * ROPE])
        wkn = at("wkn", RH + 8192, [P, HEADS * NOPE])
        wv = at("wv", RH + 10240, [P, HEADS * VD])
        cqT = at("cqT", RH + 12288, [P, 2, SEQ])
        ckvT = at("ckvT", RH + 16384, [P, SEQ])
        PT = at("PT", RH, [P, 2, NT, SEQ])
        Bn = at("Bn", RH, [P, 2, GROUPS, STATE])
        xd = at("xd", RH + 2048, [P, 2, SSDW])
        xdd = at("xdd", RH + 6144, [P, 2, SSDW])
        hst = at("hst", RH + 10240, [P, SSDW])
        htmp = at("htmp", RH + 12288, [P, SSDW])
        yt = at("yt", RH + 14336, [P, SSDW])
        ydx = at("ydx", RH + 16384, [P, SSDW])
        COS = at("COS", RI, [P, SEQ])
        SIN = at("SIN", RI + 2048, [P, SEQ])
        acc2 = at("acc2", RJ, [P, 2, SEQ])
        ropeS = at("ropeS", RJ, [P, SEQ])
        ropeR = at("ropeR", RJ + 2048, [P, SEQ])
        biasB = at("biasB", RE, [P, 3 * DFF], F32R)
        biasR = at("biasR", RE + 12288, [P, 3 * DFF])
        gffn = at("gffn", RE + 24576, [P, DM])
        gfin = at("gfin", RE + 28672, [P, DM])
        eq = at("eq", RI, [P, NT * TOPK, NE])
        eqg = at("eqg", RI + 2048, [P, NT * TOPK, NE])
        XT_hi = at("XT_hi", RA, [P, KD, P], F32R)
        XT_lo = at("XT_lo", RA + 4096, [P, KD, P], F32R)
        HT_hi = at("HT_hi", RA + 8192, [P, KD, P], F32R)
        HT_lo = at("HT_lo", RA + 12288, [P, KD, P], F32R)
        gc = at("gc", RA + 16384, [P, 2, 512])
        sg = at("sg", RA + 20480, [P, 2, 512])
        uc = at("uc", RA + 24576, [P, 2, 512])
        Xg = at("Xg", RA + 28672, [P, DM])
        ysb = at("ysb", RF, [P, DM])
        onehot = at("onehot", RF + 4096, [P, NT, P], BF16)
        gsc = at("gsc", RJ + 3104, [P, NT, NE])
        sel_gu = at("sel_gu", RF + 6144, [P, P], F32R)
        sel_dn = at("sel_dn", RF + 6656, [P, P], F32R)
        fin = at("fin", RC, [P, NT, DM])
        fsq = at("fsq", RD, [P, DM])

        spot = [RK]

        def small(name, shape, dt=F32):
            n = int(np.prod(shape[1:])) * (2 if dt == BF16 else 4)
            t = at(name, spot[0], shape, dt)
            spot[0] += (n + 31) // 32 * 32
            return t

        ident = small("ident", [P, P])
        Uinc = small("Uinc", [P, P])
        onesf = small("onesf", [P, P])
        iota_f = small("iota_f", [P, P])
        Ustrict = at("Ustrict", RJ + 2560, [P, P], BF16)
        onesb = small("onesb", [P, P], BF16)
        identb = small("identb", [P, P], BF16)
        maskA = small("maskA", [P, P], BF16)
        maskS = small("maskS", [P, P], BF16)
        vecT = small("vecT", [P, 64])
        esel = small("esel", [P, PADE])
        wrt = small("wrt", [P, KD, NE])
        brt = small("brt", [P, NE])
        dtb = small("dtb", [P, HEADS])
        alog = small("alog", [P, HEADS])
        dsk = small("dsk", [P, HEADS])
        dt = small("dt", [P, NT, HEADS])
        dtx = small("dtx", [P, NT, HEADS])
        adt = small("adt", [P, NT, HEADS])
        nacum = small("nacum", [P, NT, HEADS])
        eacum = small("eacum", [P, NT, HEADS])
        dte = small("dte", [P, NT, HEADS])
        cdec = small("cdec", [P, NT, HEADS])
        frq = small("frq", [P, 2])
        ss = small("ss", [P, 32])
        rstd = small("rstd", [P, 32])
        nmax = small("nmax", [P, 32])
        rsum = small("rsum", [P, 32])
        smid = small("smid", [P, 4])
        cntf = small("cntf", [P, 2])
        cnti = small("cnti", [P, 2], I32)
        idx_g = small("idx_g", [P, 1], I32)
        idx_s = small("idx_s", [P, 1], I32)
        idx_f = small("idx_f", [P, 1])
        vecs = at("vecs", RE + 4096, [55, P])
        posi = at("posi", RG, [P, SEQ], I32)
        posf = at("posf", RG + 2048, [P, SEQ])
        angk = at("angk", RG + 4096, [P, SEQ])
        ang = at("ang", RG + 6144, [P, SEQ])
        TG = at("TG", RJ, [P, NT, PADE, 6], BF16)
        rank = at("rank", RJ + 1664, [P, NT, PADE])
        lgt = at("lgt", RJ + 3104, [P, NT, NE])
        idxT = at("idxT", RJ + 3616, [P, PADE], I32)
        gwT = at("gwT", RJ + 3776, [P, PADE])
        mhalf = small("mhalf", [P, 4])
        krf = at("krf", RD + 4096, [ROPE, SEQ])
        junk = at("junk", RE, [P, 512])
        xjunk = at("xjunk", RC, [P, DM])
        x2junk = at("x2junk", RD, [P, DM])
        yjunk = at("yjunk", RI, [P, 256])
        kint = at("kint", RE + 2048, [P, P], I32)
        gsum = small("gsum", [P, NT])
        mask = small("mask", [P, NT, NE])
        maskb = small("maskb", [P, NT, NE], BF16)
        top8 = small("top8", [P, NT, 8])
        topi = small("topi", [P, NT, 8], U32)
        topf = small("topf", [P, NT, TOPK])
        gate = small("gate", [P, NT, TOPK])
        assert base + spot[0] <= nc.sbuf_usable_end, (base + spot[0], nc.sbuf_usable_end)

        ps = ctx.enter_context(nc.psum_tensor("ps", [P, 8, 512], F32))

        acc_d = nc.dram_tensor("acc_rows", (SEQ + P, DM), F32).ap()
        h2_d = nc.dram_tensor("h2_rows", (SEQ, DM), F32).ap()

        names = """hi_done lo_dve lo_pool split_used vec_in par_in pos_in wq_in wr_in bias_in gn_in xr_in h2_out
            acc_out out_done konst_ok pad_ok iota_ok tg_ok vec_tr vec_ok xsq xs_ok x_tr hT_hi_ok hT_lo_ok lat_sq
            lat_ok u_ok conv_ok xbc_ok sz_ok dt_in dt_e adt_ok trig_in trig_ok mla_pe mla_act mla_dve kr_sum
            kr_act kr_dve s_done nm_done exp_done pt_done pt_act pv_done yatt_hi yatt_lo pn_done cum_pe cum_act
            cum_dve xb_tr xn_ok bn_ok xd_ok xdd_ok r_pe dm_ok mm_ok yd_pe yo_pe st_pe hm_ok h_ok y1_ok y2_ok ysq
            y_rms yssd yT_pe yT_hi yT_lo x2_ok x2sq h2_ok h2t_pe h2t_act lg_pe ge_in ge_ok mask_ok rank_pe
            route_ok bias_zero bias_hi bias_lo dve_own pool_own oh_ok disp_pe disp_t idx_ok x_got xt_pe xt_hi
            xt_lo selg_ok seld_ok gub_pe gc_ok uc_ok sg_ok t_ok h_act ht_pe ht_hi ht_lo dnb_pe y_ok y_added
            rank_ok fsq_ok fo_ok x_rms lat_rms x2_rms f_rms all_added x2_pe ydx_ok rows_asked rows_sent""".split()
        (hi_done, lo_dve, lo_pool, split_used, vec_in, par_in, pos_in, wq_in, wr_in, bias_in, gn_in, xr_in,
         h2_out, acc_out, out_done, konst_ok, pad_ok, iota_ok, tg_ok, vec_tr, vec_ok, xsq, xs_ok, x_tr,
         hT_hi_ok, hT_lo_ok, lat_sq, lat_ok, u_ok, conv_ok, xbc_ok, sz_ok, dt_in, dt_e, adt_ok, trig_in,
         trig_ok, mla_pe, mla_act, mla_dve, kr_sum, kr_act, kr_dve, s_done, nm_done, exp_done, pt_done, pt_act,
         pv_done, yatt_hi, yatt_lo, pn_done, cum_pe, cum_act, cum_dve, xb_tr, xn_ok, bn_ok, xd_ok, xdd_ok, r_pe,
         dm_ok, mm_ok, yd_pe, yo_pe, st_pe, hm_ok, h_ok, y1_ok, y2_ok, ysq, y_rms, yssd, yT_pe, yT_hi, yT_lo,
         x2_ok, x2sq, h2_ok, h2t_pe, h2t_act, lg_pe, ge_in, ge_ok, mask_ok, rank_pe, route_ok, bias_zero,
         bias_hi, bias_lo, dve_own, pool_own, oh_ok, disp_pe, disp_t, idx_ok, x_got, xt_pe, xt_hi, xt_lo,
         selg_ok, seld_ok, gub_pe, gc_ok, uc_ok, sg_ok, t_ok, h_act, ht_pe, ht_hi, ht_lo, dnb_pe, y_ok, y_added,
         rank_ok, fsq_ok, fo_ok, x_rms, lat_rms, x2_rms, f_rms, all_added, x2_pe, ydx_ok, rows_asked, rows_sent) = (sem(n) for n in names)
        raw_in = [sem(f"raw_in{k}") for k in range(RAW)]
        xraw_in = [sem(f"xraw_in{k}") for k in range(XRAW)]
        x_in = [sem(f"x_in{j}") for j in range(NT)]
        fin_in = [sem(f"fin_in{j}") for j in range(NT)]

        block = ctx.enter_context(nc.Block())

        w_in, w_out = A["w_in"][0], A["w_out"][0]
        w_gu = A["w_gate_up"][0].rearrange("e (k p) n -> e k p n", p=P)
        w_dn = A["w_down"][0].rearrange("e (c k p) n -> e c p k n", p=P, k=2)

        IN_COLS = [(SSDW + 2 * SSDW, SMALL), (SSDW, SSDW), (2 * SSDW, SSDW), (0, SSDW)]

        def xraw(k):
            k = k % XRAW
            return raw[:, k, :] if k < RAW else raw_more[:, k - RAW, :]

        class Chain:

            def __init__(self, eng, s):
                self.eng, self.s, self.n = eng, s, 0

            def __call__(self, ins):
                ins.then_inc(self.s, 1)
                self.n += 1
                self.eng.wait_ge(self.s, self.n)

        def past(n):
            return n + 1

        def heads(t, n):
            return t.unsqueeze(2).to_broadcast([P, HEADS, n])

        def mla_evacuated(eng, i):
            mine = sum(1 for v in range(i + 1) if MLA[v][2] == MLA[i][2])
            eng.wait_ge(mla_act if MLA[i][2] == "A" else mla_dve, mine)

        def more_passes(eng, one_pass):
            eng.wait_ge(route_ok, 1)
            most = eng.value_load(cnti[0:1, 0:1], min_val=0, max_val=SEQ)
            with eng.If(most > P):
                with eng.Fori(1, SEQ // P) as r:
                    with eng.If(most > r * P):
                        one_pass(r)

        @block.sync
        def _(sp):
            for j in range(NT):
                sp.dma_start(xnat[:, j, :], A["x"][0, j * P:(j + 1) * P, :]).then_inc(x_in[j], 16)

            rows_of = lambda t: t.rearrange("(k p) -> k p", p=P)
            sp.dma_start(vecs[0:8, :], rows_of(A["norm_mix_g"][0])).then_inc(vec_in, 16)
            sp.dma_start(vecs[8:40, :], A["conv_w"][0].rearrange("w (k p) -> (w k) p", p=P)).then_inc(vec_in, 16)
            sp.dma_start(vecs[40:48, :], rows_of(A["conv_b"][0])).then_inc(vec_in, 16)
            sp.dma_start(vecs[48:50, :], rows_of(A["q_norm_g"][0])).then_inc(vec_in, 16)
            sp.dma_start(vecs[50:51, :], rows_of(A["kv_norm_g"][0])).then_inc(vec_in, 16)
            sp.dma_start(vecs[51:55, :], rows_of(A["ssd_norm_g"][0])).then_inc(vec_in, 16)

            def small_loads():
                sp.dma_start(posi[:, :], A["positions"][0].partition_broadcast(P)).then_inc(pos_in, 16)
                sp.dma_start(frq[:, :], A["rope_freq"]).then_inc(pos_in, 16)
                sp.dma_start(dtb[:, :], A["dt_bias"][0].partition_broadcast(P)).then_inc(par_in, 16)
                sp.dma_start(alog[:, :], A["a_log"][0].partition_broadcast(P)).then_inc(par_in, 16)
                sp.dma_start(dsk[:, :], A["d_skip"][0].partition_broadcast(P)).then_inc(par_in, 16)
                per_head = lambda t: t.rearrange("p (h d) -> p h d", h=HEADS)
                for k in range(2):
                    uq = per_head(A["w_uq"][0][k * P:(k + 1) * P, :])
                    sp.dma_start(per_head(wqn[:, k, :]), uq[:, :, 0:NOPE]).then_inc(wq_in, 16)
                    sp.dma_start(per_head(wqs[:, k, :]), uq[:, :, NOPE:QK]).then_inc(wq_in, 16)
                    sp.dma_start(per_head(wqr[:, k, :])[:, :, 0:ROPE // 2], uq[:, :, NOPE + ROPE // 2:QK]).then_inc(wq_in, 16)
                    sp.dma_start(per_head(wqr[:, k, :])[:, :, ROPE // 2:ROPE], uq[:, :, NOPE:NOPE + ROPE // 2]).then_inc(wq_in, 16)
                ukv = per_head(A["w_ukv"][0])
                sp.dma_start(per_head(wkn[:, :]), ukv[:, :, 0:NOPE]).then_inc(wq_in, 16)
                sp.dma_start(per_head(wv[:, :]), ukv[:, :, NOPE:NOPE + VD]).then_inc(wq_in, 16)
                sp.dma_start(wrt[:, :, :], A["w_router"][0].rearrange("(k p) n -> p k n", p=P)).then_inc(wr_in, 16)
                sp.dma_start(brt[:, :], A["b_router"][0].partition_broadcast(P)).then_inc(wr_in, 16)

            def load(slot, src, free, width=CHUNK, k=1):
                if free is not None:
                    sp.wait_ge(lo_dve, free)
                    sp.wait_ge(lo_pool, free)
                sp.dma_start(raw[:, slot, 0:width].rearrange("p (k n) -> p k n", k=k), src).then_inc(raw_in[slot], 16)

            for n in range(IN_CHUNKS):
                if n == RAW:
                    small_loads()
                c0, w = IN_COLS[n // 2]
                rows = w_in[(n % 2) * 4 * P:(n % 2 + 1) * 4 * P, c0:c0 + w].rearrange("(k p) n -> p k n", p=P)
                load(n % RAW, rows, n - RAW + 1 if n >= RAW else None, 4 * w, 4)
            for c in range(OUT_CHUNKS):
                n = IN_CHUNKS + c
                k = OUT_ORDER[2 * c]
                rows = w_out[k * P:(k + 2) * P, :].rearrange("(k p) n -> p k n", p=P)
                load(n % RAW, rows, n - RAW + 1, CHUNK, 2)

            def load_x(n0, k, src, parts, free=XRAW):
                if free:
                    sp.wait_ge(lo_dve, n0 + (k - free + 1))
                    sp.wait_ge(lo_pool, n0 + (k - free + 1))
                sp.dma_start(xraw(k).rearrange("p (k n) -> p k n", k=parts), src).then_inc(xraw_in[k % XRAW], 16)

            def gate_up(e, n0, k0, part=range(GUC), free=XRAW):
                for c in part:
                    load_x(n0, k0 + c, w_gu[bass.ds(e, 1), c].rearrange("a p n -> p a n"), 1, free)

            def down(e, n0, k0):
                for c in range(DNC):
                    load_x(n0, k0 + c, w_dn[bass.ds(e, 1), c].rearrange("a p k n -> p (a k) n"), 2)

            def one_pass(r):
                with sp.Fori(1, NE) as e:
                    n0 = r * PASS + e * EC
                    gate_up(e, n0, N0 + GUC - EC)
                    down(e - 1, n0, N0 + 2 * GUC - EC)
                down(NE - 1, r * PASS, N0 + PASS - DNC)

            gate_up(0, 0, N0, range(RAW), free=RAW)
            for j in range(NT):
                sp.wait_ge(x2_ok, j + 1)
                sp.dma_start(acc_d[j * P:(j + 1) * P, :], x2[:, j, :]).then_inc(acc_out, 16)
            for j in range(NT):
                sp.wait_ge(h2_ok, j + 1)
                sp.dma_start(h2_d[j * P:(j + 1) * P, :], h2[:, j, :]).then_inc(h2_out, 16)
            sp.wait_ge(x2sq, NT)
            sp.wait_ge(acc_out, 16 * NT)
            gate_up(0, 0, N0, range(RAW, XRAW), free=0)
            gate_up(0, 0, N0, range(XRAW, GUC))
            one_pass(0)
            more_passes(sp, lambda r: (gate_up(0, r * PASS, N0), one_pass(r)))
            sp.wait_ge(all_added, 1)
            for j in range(NT):
                sp.dma_start(fin[:, j, :], acc_d[j * P:(j + 1) * P, :]).then_inc(fin_in[j], 16)
            for j in range(NT):
                sp.wait_ge(fo_ok, j + 1)
                sp.dma_start(out[0, j * P:(j + 1) * P, :], fin[:, j, :]).then_inc(out_done, 16)
            sp.wait_ge(out_done, 16 * NT)

        @block.tensor
        def _(pe):
            T = nc.tensor

            def high_ready(n):
                pe.wait_ge(hi_done, n + 1)

            def low_ready(n):
                pe.wait_ge(lo_dve, n + 1)
                pe.wait_ge(lo_pool, n + 1)

            pe.wait_ge(konst_ok, 1)
            pe.wait_ge(vec_in, 6 * 16)
            T.transpose(ps[:, 7, 0:55], vecs[:, :], ident[0:55, 0:55]).then_inc(vec_tr, 1)
            pe.wait_ge(vec_ok, 1)
            for j in range(NT):
                pe.wait_ge(xs_ok, j + 1)
                for k in range(KD):
                    ins = T.transpose(ps[:, k, j * P:(j + 1) * P], xnat[:, j, k * P:(k + 1) * P], ident[:, :])
                    if j == NT - 1:
                        ins.then_inc(x_tr, 1)

            for b in range(4):
                w = IN_COLS[b][1]
                bank0 = 4 * (b % 2)
                if b == 2:
                    pe.wait_ge(lat_sq, 2 * NT)
                    pe.wait_ge(lat_ok, NT)
                if b == 3:
                    pe.wait_ge(u_ok, 4)
                for half in range(2):
                    n = 2 * b + half
                    Wh = whi[:, n % SPL, 0:4 * w].rearrange("p (k n) -> p k n", k=4)
                    Wl = wlo[:, n % SPL, 0:4 * w].rearrange("p (k n) -> p k n", k=4)
                    if b == 0:
                        pe.wait_ge(hT_hi_ok, 4 * (half + 1))
                        pe.wait_ge(hT_lo_ok, 4 * (half + 1))
                    high_ready(n)
                    low_ready(n)
                    for kk in range(4):
                        k = 4 * half + kk
                        ah, al = actT_hi[:, k, :], actT_lo[:, k, :]
                        for m in range(4):
                            tm = slice(m * P, (m + 1) * P)
                            if b in (0, 3):
                                trio = ((ah[:, tm], Wh[:, kk, :]), (al[:, tm], Wh[:, kk, :]), (ah[:, tm], Wl[:, kk, :]))
                            else:
                                trio = ((Wh[:, kk, tm], ah), (Wh[:, kk, tm], al), (Wl[:, kk, tm], ah))
                            for q, (l, r) in enumerate(trio):
                                ins = T.matmul(ps[:, bank0 + m, 0:w], l, r, start=k == 0 and q == 0, stop=k == 7 and q == 2)
                    ins.then_inc(split_used, 1)

            for i, (kind, a, _) in enumerate(MLA):
                o = ps[:, i % 8, :]
                if i < 4:
                    pe.wait_ge(u_ok, 5 + i)
                elif i < 8:
                    pe.wait_ge(sz_ok, i - 3)
                else:
                    mla_evacuated(pe, i - 8)
                if kind == "lat":
                    for j in range(NT):
                        ins = T.transpose(o[:, j * P:(j + 1) * P], latn[:, j, a * P:(a + 1) * P], ident[:, :])
                elif kind == "kr":
                    for j in range(NT):
                        ins = T.transpose(o[0:ROPE, j * P:(j + 1) * P], krn[:, j, a, :], ident[:, :])
                elif kind in ("qn", "qs", "qr"):
                    if i == 5:
                        pe.wait_ge(wq_in, 16 * WQ)
                        mla_evacuated(pe, 0)
                        mla_evacuated(pe, 1)
                    for kk in range(2):
                        l = {"qn": wqn, "qs": wqs, "qr": wqr}[kind][:, kk, a * P:(a + 1) * P]
                        ins = T.matmul(o, l, cqT[:, kk, :], start=kk == 0, stop=kk == 1)
                elif kind == "kn":
                    mla_evacuated(pe, 2)
                    ins = T.matmul(o, wkn[:, a * P:(a + 1) * P], ckvT[:, :], start=True, stop=True)
                else:
                    ins = T.matmul(o, ckvT[:, a * P:(a + 1) * P], wv[:, :], start=True, stop=True)
                ins.then_inc(mla_pe, 1)
            def scores(u):
                h, i = u // NT, u % NT
                w = (i + 1) * P
                b = S_BANK[u % 4]
                if u >= 4:
                    pe.wait_ge(exp_done, u - 3)
                T.matmul(ps[:, b, 0:w], QT[0:QK, h, i * P:w], KT[0:QK, h, 0:w], start=True, stop=False)
                T.matmul(ps[:, b, i * P:w], identb[:, :], maskA[:, :], start=False, stop=True).then_inc(s_done, 1)

            def pt_copied(u):
                pe.wait_ge(pt_act, u + 1)

            def outputs(h):
                m, rows = h // 2, slice(VD * (h % 2), VD * (h % 2) + VD)
                pt_copied(NT * h + NT - 2)
                pt_copied(NT * h + NT - 1)
                if h % 2 == 0 and m >= 2:
                    pe.wait_ge(yatt_hi, m - 1)
                    pe.wait_ge(yatt_lo, m - 1)
                for kk in range(NT):
                    ins = T.matmul(ps[rows, 4 + m % 2, kk * P:], V[:, kk, h * VD:(h + 1) * VD],
                                   PT[:, h % 2, kk, kk * P:], start=kk == 0, stop=kk == NT - 1)
                ins.then_inc(pv_done, 1)

            mla_evacuated(pe, 12)
            mla_evacuated(pe, 14)
            pe.wait_ge(kr_act, 1)
            pe.wait_ge(kr_dve, 1)
            scores(0)
            mla_evacuated(pe, 15)
            scores(1)
            mla_evacuated(pe, 16)
            scores(2)
            for i in (17, 18, 19, 20):
                mla_evacuated(pe, i)
            for u in range(NU):
                pe.wait_ge(pn_done, u + 1)
                if u >= 2:
                    pt_copied(u - 2)
                for kk in range(u % NT + 1):
                    ins = T.transpose(ps[:, 2 + u % 2, kk * P:(kk + 1) * P], Pr[:, u % 4, kk * P:(kk + 1) * P], ident[:, :])
                ins.then_inc(pt_done, 1)
                if u + 3 < NU:
                    scores(u + 3)
                if u >= NT and u % NT == 1:
                    outputs(u // NT - 1)
            outputs(HEADS - 1)

            pe.wait_ge(adt_ok, 1)
            flat = adt[:, :, :].rearrange("p j h -> p (j h)")
            T.matmul(ps[:, 7, 0:32], Uinc[:, :], flat, start=True, stop=True)
            T.matmul(ps[:, 7, 32:64], onesf[:, :], flat, start=True, stop=True).then_inc(cum_pe, 1)
            pe.wait_ge(yatt_hi, 3)
            pe.wait_ge(yatt_lo, 3)
            pe.wait_ge(xbc_ok, 8)
            for j in range(NT):
                tj = slice(j * P, (j + 1) * P)
                if j >= 1:
                    pe.wait_ge(xn_ok, j)
                    pe.wait_ge(bn_ok, j)
                    pe.wait_ge(mm_ok, 2 * j)
                for m in range(4):
                    T.transpose(ps[:, 0, m * P:(m + 1) * P], XBC[:, m, tj], ident[:, :])
                for g in range(GROUPS):
                    T.transpose(ps[:, 1, g * P:(g + 1) * P], XBC[:, 4 + g, tj], ident[:, :])
                for g in range(GROUPS):
                    ins = T.matmul(ps[:, 1, (2 + g) * P:(3 + g) * P], XBC[:, 4 + g, tj], XBC[:, 6 + g, tj],
                                   start=True, stop=True)
                ins.then_inc(xb_tr, 1)
                for g in range(GROUPS):
                    if j >= 1:
                        pe.wait_ge(dm_ok, 2 * (j - 1) + g + 1)
                    for q in range(4):
                        o = ps[:, 2 + g, q * P:(q + 1) * P]
                        h = 4 * g + q
                        T.matmul(o, adt[:, j, h:h + 1].to_broadcast([P, P]), Uinc[:, :], start=True, stop=False)
                        ins = T.matmul(o, identb[:, :], maskS[:, :], start=False, stop=True)
                    ins.then_inc(r_pe, 1)
                if j >= 1:
                    pe.wait_ge(h_ok, j)
                    if j >= 2:
                        pe.wait_ge(y1_ok, j)
                    for g in range(GROUPS):
                        ins = T.matmul(ps[:, 6, g * 256:(g + 1) * 256], XBC[:, 6 + g, tj],
                                       hst[:, g * 256:(g + 1) * 256], start=True, stop=True)
                    ins.then_inc(yo_pe, 1)
                pe.wait_ge(xd_ok, j + 1)
                if j == 1:
                    pe.wait_ge(yatt_hi, 4)
                    pe.wait_ge(yatt_lo, 4)
                if j >= 2:
                    pe.wait_ge(y1_ok, j - 1)
                for g in range(GROUPS):
                    pe.wait_ge(mm_ok, 2 * j + g + 1)
                    for q in range(4):
                        h = 4 * g + q
                        ins = T.matmul(ps[:, 4 + j % 2, h * HD:(h + 1) * HD], Mm[:, g, q, :],
                                       xd[:, j % 2, h * HD:(h + 1) * HD], start=True, stop=True)
                ins.then_inc(yd_pe, 1)
                if j < NT - 1:
                    pe.wait_ge(xdd_ok, j + 1)
                    pe.wait_ge(bn_ok, j + 1)
                    if j == 0:
                        pe.wait_ge(cum_dve, 2)
                        pe.wait_ge(cum_act, 2)
                    for g in range(GROUPS):
                        ins = T.matmul(ps[:, 7, g * 256:(g + 1) * 256], Bn[:, j % 2, g, :],
                                       xdd[:, j % 2, g * 256:(g + 1) * 256], start=True, stop=True)
                    ins.then_inc(st_pe, 1)

            def split_of(t, c):
                return t[:, (IN_CHUNKS + c) % SPL, :].rearrange("p (k n) -> p k n", k=2)

            def project(c, kk, j):
                k = OUT_ORDER[2 * c + kk]
                for q, (l, W) in enumerate(((actT_hi, whi), (actT_lo, whi), (actT_hi, wlo))):
                    for f in range(2):
                        ins = T.matmul(ps[:, 2 * j + f, :], l[:, slot_of(k), j * P:(j + 1) * P],
                                       split_of(W, c)[:, kk, f * 512:(f + 1) * 512],
                                       start=c == 0 and kk == 0 and q == 0, stop=c == OUT_CHUNKS - 1 and kk == 1 and q == 2)
                return ins

            def ssd_features(f):
                for j in range(NT):
                    ins = T.transpose(ps[:, 6 + f % 2, j * P:(j + 1) * P], Ynat[:, j, f * P:(f + 1) * P], ident[:, :])
                ins.then_inc(yT_pe, 1)

            pe.wait_ge(y1_ok, NT)
            pe.wait_ge(yatt_hi, 4)
            pe.wait_ge(yatt_lo, 4)
            for c in range(2):
                high_ready(IN_CHUNKS + c)
                low_ready(IN_CHUNKS + c)
                for kk in range(2):
                    if c == 1:
                        if kk == 0:
                            pe.wait_ge(yssd, NT)
                        else:
                            pe.wait_ge(yT_hi, 2)
                            pe.wait_ge(yT_lo, 2)
                        ssd_features(2 * kk)
                        ssd_features(2 * kk + 1)
                    for j in range(NT - 1):
                        project(c, kk, j)
            pe.wait_ge(yT_hi, 4)
            pe.wait_ge(yT_lo, 4)
            for c in range(2):
                for kk in range(2):
                    ins = project(c, kk, NT - 1)
                ins.then_inc(split_used, 1)
            for c in range(2, OUT_CHUNKS):
                high_ready(IN_CHUNKS + c)
                low_ready(IN_CHUNKS + c)
                if c < OUT_CHUNKS - 1:
                    for kk in range(2):
                        for j in range(NT):
                            ins = project(c, kk, j)
                else:
                    for j in range(NT):
                        for kk in range(2):
                            ins = project(c, kk, j)
                        if j < NT - 1:
                            ins.then_inc(x2_pe, 1)
                ins.then_inc(split_used, 1)

            def h2_features(j):
                pe.wait_ge(h2_ok, j + 1)
                for k in range(KD):
                    ins = T.transpose(ps[:, 2 * j + k // 4, (k % 4) * P:(k % 4 + 1) * P], h2[:, j, k * P:(k + 1) * P], ident[:, :])
                ins.then_inc(h2t_pe, 1)

            def logits(j):
                pe.wait_ge(h2t_act, j + 1)
                for k in range(KD):
                    ins = T.matmul(ps[:, 2 * j, 0:NE], h2T[:, j, k, :], wrt[:, k, :], start=k == 0, stop=k == KD - 1)
                ins.then_inc(lg_pe, 1)

            pe.wait_ge(wr_in, 32)
            h2_features(0)
            for j in range(1, NT):
                h2_features(j)
                logits(j - 1)
            logits(NT - 1)
            pe.wait_ge(mask_ok, 1)
            pe.wait_ge(tg_ok, 2)
            for j in range(NT):
                for i in range(j + 1):
                    T.matmul(ps[:, 1, j * NE:(j + 1) * NE], Ustrict[:, :] if i == j else onesb[:, :], maskb[:, i, :],
                             start=i == 0, stop=i == j)
            for i in range(NT):
                ins = T.matmul(ps[:, 3, 0:NE], onesb[:, :], maskb[:, i, :], start=i == 0, stop=i == NT - 1)
            ins.then_inc(rank_pe, 1)

            def dispatch(D, e, bank=6):
                pe.wait_ge(oh_ok, D + 1)
                for j in range(NT):
                    ins = T.matmul(ps[:, bank, 0:6], onehot[:, j, :], TG[:, j, bass.ds(e, 1), :].rearrange("p a c -> p (a c)"),
                                   start=j == 0, stop=j == NT - 1)
                ins.then_inc(disp_pe, 1)

            def rows(D, tables):
                pe.wait_ge(x_got, 16 * (D + 1))
                pe.wait_ge(idx_ok, tables)
                for k in range(KD):
                    ins = T.transpose(ps[:, 6 + k // 4, (k % 4) * P:(k % 4 + 1) * P], Xg[:, k * P:(k + 1) * P], ident[:, :])
                ins.then_inc(xt_pe, 1)

            def gate_up(E, X, D, e, n0, k0):
                pe.wait_ge(selg_ok, X + 1)
                pe.wait_ge(uc_ok, past(2 * E))
                for m in range(4):
                    ins = T.matmul(ps[:, m, :], sel_gu[:, :], biasB[:, m * 512:(m + 1) * 512], start=True, stop=False)
                ins.then_inc(gub_pe, 1)
                pe.wait_ge(xt_hi, X + 1)
                pe.wait_ge(xt_lo, X + 1)
                for c in range(GUC):
                    if c == 4:
                        pe.wait_ge(ht_hi, past(E))
                        pe.wait_ge(ht_lo, past(E))
                        dispatch(D + 2, e + 2)
                    s = (k0 + c) % SPL
                    high_ready(n0 + (k0 + c))
                    for l in (XT_hi, XT_lo):
                        for m in range(4):
                            T.matmul(ps[:, m, :], l[:, c, :], whi[:, s, m * 512:(m + 1) * 512], start=False, stop=False)
                    low_ready(n0 + (k0 + c))
                    for m in range(4):
                        ins = T.matmul(ps[:, m, :], XT_hi[:, c, :], wlo[:, s, m * 512:(m + 1) * 512],
                                       start=False, stop=c == GUC - 1)
                    ins.then_inc(split_used, 1)

            def down(E, n0, k0):
                pe.wait_ge(seld_ok, E + 1)
                pe.wait_ge(y_ok, past(E))
                for m in range(2):
                    ins = T.matmul(ps[:, 4 + m, :], sel_dn[:, :], biasB[:, (4 + m) * 512:(5 + m) * 512], start=True, stop=False)
                ins.then_inc(dnb_pe, 1)
                pe.wait_ge(ht_hi, past(E + 1))
                pe.wait_ge(ht_lo, past(E + 1))
                for c in range(DNC):
                    s = (k0 + c) % SPL
                    high_ready(n0 + (k0 + c))
                    for kk in range(2):
                        for l in (HT_hi, HT_lo):
                            for m in range(2):
                                T.matmul(ps[:, 4 + m, :], l[:, 2 * c + kk, :],
                                         whi[:, s, kk * DM + m * 512:kk * DM + (m + 1) * 512], start=False, stop=False)
                    low_ready(n0 + (k0 + c))
                    for kk in range(2):
                        for m in range(2):
                            ins = T.matmul(ps[:, 4 + m, :], HT_hi[:, 2 * c + kk, :],
                                           wlo[:, s, kk * DM + m * 512:kk * DM + (m + 1) * 512],
                                           start=False, stop=c == DNC - 1 and kk == 1)
                    ins.then_inc(split_used, 1)

            def hidden(E, X):
                pe.wait_ge(h_act, 2 * E + 2)
                pe.wait_ge(xt_hi, X)
                pe.wait_ge(xt_lo, X)
                for k in range(KD):
                    ins = T.transpose(ps[:, 6 + k // 4, (k % 4) * P:(k % 4 + 1) * P],
                                      uc[:, k // 4, (k % 4) * P:(k % 4 + 1) * P], ident[:, :])
                ins.then_inc(ht_pe, 1)

            pe.wait_ge(bias_lo, 1)

            def one_pass(r):
                E0, X0, D0 = r * NE, r * (NE + 1), r * PADE
                pe.wait_ge(ht_hi, past(E0))
                pe.wait_ge(ht_lo, past(E0))
                dispatch(D0, 0)
                pe.wait_ge(y_ok, past(E0))
                dispatch(D0 + 1, 1, bank=5)
                rows(D0, D0 + 1)
                gate_up(E0, X0, D0, 0, r * PASS, N0)
                rows(D0 + 1, D0 + 3)
                hidden(E0, X0 + 2)
                with pe.Fori(1, NE) as e:
                    E, X, D, n0 = E0 + e, X0 + e, D0 + e, r * PASS + e * EC
                    gate_up(E, X, D, e, n0, N0 + GUC - EC)
                    rows(D + 1, D + 3)
                    down(E - 1, n0, N0 + 2 * GUC - EC)
                    hidden(E, X + 2)
                down(E0 + (NE - 1), r * PASS, N0 + PASS - DNC)

            one_pass(0)
            more_passes(pe, one_pass)

        @block.scalar
        def _(act):
            S = nc.scalar
            def high(n):
                if n >= SPL:
                    act.wait_ge(split_used, n - SPL + 1)
                act.wait_ge(raw_in[n % RAW], 16 * (n // RAW + 1))
                w = block_of(n)[0]
                S.activation(whi[:, n % SPL, 0:w], raw[:, n % RAW, 0:w], ACT.Copy).then_inc(hi_done, 1)

            for j in range(NT):
                act.wait_ge(x_in[j], 16)
                if j:
                    act.wait_ge(xsq, j)
                S.activation(xjunk[:, :], xnat[:, j, :], ACT.Square, accum_out=ss[:, j:j + 1]).then_inc(xsq, 1)
            act.wait_ge(vec_tr, 1)
            S.activation(vecT[:, 0:48], ps[:, 7, 0:48], ACT.Copy)
            S.activation(vecT[:, 48:50], ps[:, 7, 48:50], ACT.Copy, scale=-SCALE)
            S.activation(vecT[:, 50:55], ps[:, 7, 50:55], ACT.Copy).then_inc(vec_ok, 1)
            high(0)
            high(1)
            act.wait_ge(vec_ok, 1)
            for k in range(KD):
                act.wait_ge(x_tr, k + 1)
                S.activation(actT_hi[:, k, :], ps[:, k, :], ACT.Copy, scale=vecT[:, k:k + 1]).then_inc(hT_hi_ok, 1)
            high(2)
            act.wait_ge(trig_in, 2)
            S.activation(COS[:, :], ang[:, :], ACT.Sin)
            S.activation(SIN[:, :], angk[:, :], ACT.Sin, scale=frq[:, 1:2]).then_inc(trig_ok, 1)
            high(3)
            high(4)
            act.wait_ge(split_used, 2)
            for j in range(NT):
                if j:
                    act.wait_ge(lat_sq, 2 * j)
                S.activation(junk[:, 0:QR], ps[:, j, 8:8 + QR], ACT.Square, accum_out=ss[:, 4 + j:5 + j]).then_inc(lat_sq, 1)
                S.activation(junk[:, QR:QR + KVR], ps[:, j, 8 + QR:8 + QR + KVR], ACT.Square,
                             accum_out=ss[:, 8 + j:9 + j]).then_inc(lat_sq, 1)
            act.wait_ge(dt_in, 1)
            S.activation(dtx[:, :, :], dt[:, :, :], ACT.Abs).then_inc(dt_e, 1)
            act.wait_ge(dt_e, 1)
            S.activation(dtx[:, :, :], dtx[:, :, :], ACT.Exp, scale=-1.0).then_inc(dt_e, 1)
            act.wait_ge(par_in, 48)
            S.activation(alog[:, :], alog[:, :], ACT.Exp)
            act.wait_ge(dt_e, 2)
            S.activation(dtx[:, :, :], dtx[:, :, :], ACT.Ln, bias=1.0).then_inc(dt_e, 1)
            high(5)

            def window(m):
                if m >= 4:
                    act.wait_ge(conv_ok, m - 3)
                S.activation(U[:, m % 4, 3:3 + SEQ], ps[:, (4 if m < 4 else 0) + m % 4, :], ACT.Copy).then_inc(u_ok, 1)

            def channels(m):
                act.wait_ge(conv_ok, m + 1)
                S.activation(XBC[:, m, :], acc2[:, m % 2, :], ACT.Silu, bias=vecT[:, 40 + m:41 + m]).then_inc(xbc_ok, 1)

            act.wait_ge(split_used, 4)
            for m in range(4):
                window(m)
            high(6)
            for m in range(4):
                channels(m)
            high(7)
            act.wait_ge(split_used, 6)
            for m in range(4, 8):
                window(m)
            high(8)
            for m in range(4, 8):
                channels(m)
            act.wait_ge(split_used, 8)
            for j in range(NT):
                S.activation(sz[:, j, :], ps[:, 4 + j, :], ACT.Silu).then_inc(sz_ok, 1)

            for i, (kind, a, eng) in enumerate(MLA):
                if eng != "A":
                    continue
                b = i % 8
                act.wait_ge(mla_pe, i + 1)
                if kind == "lat":
                    dst = cqT[:, a, :] if a < 2 else ckvT[:, :]
                    S.activation(dst, ps[:, b, :], ACT.Copy, scale=vecT[:, 48 + a:49 + a]).then_inc(mla_act, 1)
                elif kind in ("qn", "kn"):
                    dst = QT if kind == "qn" else KT
                    S.activation(dst[0:NOPE, 2 * a, :], ps[0:NOPE, b, :], ACT.Copy)
                    S.activation(dst[0:NOPE, 2 * a + 1, :], ps[NOPE:P, b, :], ACT.Copy).then_inc(mla_act, 1)
                    if (kind, a) == ("qn", 2):
                        act.wait_ge(kr_sum, 1)
                        for h in range(4, HEADS):
                            ins = S.activation(KT[NOPE:QK, h, :], krf[:, :], ACT.Copy)
                        ins.then_inc(kr_act, 1)
                else:
                    S.activation(V[:, a, :], ps[:, b, :], ACT.Copy).then_inc(mla_act, 1)

            def pt_copy(u):
                h, i = u // NT, u % NT
                act.wait_ge(pt_done, u + 1)
                if h >= 2:
                    act.wait_ge(pv_done, h - 1)
                S.activation(PT[:, h % 2, 0:i + 1, i * P:(i + 1) * P],
                             ps[:, 2 + u % 2, 0:(i + 1) * P].rearrange("p (k n) -> p k n", n=P), ACT.Copy).then_inc(pt_act, 1)

            def attended(m):
                act.wait_ge(pv_done, 2 * m + 2)
                S.activation(actT_hi[:, slot_of(4 + m), :], ps[:, 4 + m % 2, :], ACT.Copy).then_inc(yatt_hi, 1)

            for u in range(NU):
                w = (u % NT + 1) * P
                act.wait_ge(nm_done, u + 1)
                if u >= 4:
                    act.wait_ge(pt_done, u - 3)
                S.activation(Pr[:, u % 4, 0:w], ps[:, S_BANK[u % 4], 0:w], ACT.Exp, bias=nmax[:, u:u + 1], scale=-1.0,
                             accum_out=rsum[:, u:u + 1]).then_inc(exp_done, 1)
                if u >= 2:
                    pt_copy(u - 2)
                if u % 8 == 5 and u > 8:
                    attended(u // 8 - 1)
                if u in (6, 14):
                    high(9 + u // 8)
            pt_copy(NU - 2)
            pt_copy(NU - 1)
            attended(HEADS // 2 - 1)

            fl = lambda t: t[:, :, :].rearrange("p j h -> p (j h)")
            act.wait_ge(cum_dve, 2)
            S.activation(fl(eacum), fl(nacum), ACT.Exp, scale=-1.0).then_inc(cum_act, 1)
            S.activation(fl(cdec), ps[:, 7, 32:64], ACT.Exp).then_inc(cum_act, 1)
            S.activation(fl(dte), fl(dtx), ACT.Exp).then_inc(cum_act, 1)

            def finish_y(j):
                act.wait_ge(y2_ok, j + 1)
                for g in range(GROUPS):
                    if 2 * j + g:
                        act.wait_ge(ysq, 2 * j + g)
                    S.activation(yjunk[:, :], Ynat[:, j, g * 256:(g + 1) * 256], ACT.Square,
                                 accum_out=ss[:, 20 + 2 * j + g:21 + 2 * j + g]).then_inc(ysq, 1)
                act.wait_ge(y_rms, j + 1)
                for g in range(GROUPS):
                    ins = S.activation(Ynat[:, j, g * 256:(g + 1) * 256], Ynat[:, j, g * 256:(g + 1) * 256], ACT.Copy,
                                       scale=rstd[:, 20 + 2 * j + g:21 + 2 * j + g])
                ins.then_inc(yssd, 1)

            for j in range(NT):
                act.wait_ge(xb_tr, j + 1)
                S.activation(Xn[:, j, :], ps[:, 0, :], ACT.Copy).then_inc(xn_ok, 1)
                if j >= 2:
                    act.wait_ge(st_pe, j - 1)
                S.activation(Bn[:, j % 2, :, :].rearrange("p g n -> p (g n)"), ps[:, 1, 0:256], ACT.Copy).then_inc(bn_ok, 1)
                for g in range(GROUPS):
                    act.wait_ge(r_pe, 2 * j + g + 1)
                    if j >= 1:
                        act.wait_ge(mm_ok, 2 * (j - 1) + g + 1)
                    for q in range(4):
                        h = 4 * g + q
                        ins = S.activation(Dm[:, g, q, :], ps[:, 2 + g, q * P:(q + 1) * P], ACT.Exp, bias=nacum[:, j, h:h + 1])
                    ins.then_inc(dm_ok, 1)
                if j >= 1:
                    finish_y(j - 1)
            finish_y(NT - 1)

            for f in range(4):
                act.wait_ge(yT_pe, f + 1)
                S.activation(actT_hi[:, slot_of(f), :], ps[:, 6 + f % 2, :], ACT.Copy, scale=vecT[:, 51 + f:52 + f]).then_inc(yT_hi, 1)
            high(11)
            act.wait_ge(bias_in, 64)
            S.activation(biasB[0:64, :], biasR[0:64, :], ACT.Copy).then_inc(bias_hi, 1)
            def high_x(n0, w0, k):
                act.wait_ge(split_used, n0 + (k - SPL + 1))
                act.wait_ge(xraw_in[k % XRAW], w0 + 16 * ((k - N0) // XRAW + 1))
                S.activation(whi[:, k % SPL, :], xraw(k), ACT.Copy).then_inc(hi_done, 1)

            def presplit(n0, w0):
                high_x(n0, w0, N0)
                high_x(n0, w0, N0 + 1)

            presplit(0, 0)
            for j in range(NT):
                act.wait_ge(x2_ok, j + 1)
                if j:
                    act.wait_ge(x2sq, j)
                S.activation(x2junk[:, :], x2[:, j, :], ACT.Square, accum_out=ss[:, 12 + j:13 + j]).then_inc(x2sq, 1)
            for j in range(NT):
                act.wait_ge(h2t_pe, j + 1)
                S.activation(h2T[:, j, :, :].rearrange("p (a k) n -> p a (k n)", a=2), ps[:, 2 * j:2 * j + 2, :],
                             ACT.Copy).then_inc(h2t_act, 1)
            act.wait_ge(ge_in, 1)
            S.activation(gate[:, :, :], gate[:, :, :], ACT.Exp).then_inc(ge_ok, 1)

            both = lambda t: t[:, :, :].rearrange("p (a k) n -> p a (k n)", a=2)

            def rows_high(X):
                act.wait_ge(xt_pe, past(X + 1))
                S.activation(both(XT_hi), ps[:, 6:8, :], ACT.Copy).then_inc(xt_hi, 1)

            def hidden_high(E):
                act.wait_ge(ht_pe, E + 1)
                S.activation(both(HT_hi), ps[:, 6:8, :], ACT.Copy).then_inc(ht_hi, 1)

            def select(e, dst, done, used, count):
                act.wait_ge(used, past(count))
                S.activation(dst[:, :], esel[:, bass.ds(e, 1)].to_broadcast([P, P]), ACT.Copy).then_inc(done, 1)

            def sigmoid(E, f):
                act.wait_ge(gc_ok, 2 * E + f + 1)
                S.activation(sg[:, f, :], gc[:, f, :], ACT.Sigmoid, scale=ALPHA).then_inc(sg_ok, 1)

            def weighted(E, e):
                act.wait_ge(y_added, 16 * past(E))
                S.activation(idx_s[:, :], idxT[:, bass.ds(e, 1)], ACT.Copy)
                S.activation(ysb[:, :].rearrange("p (a n) -> p a n", a=2), ps[:, 4:6, :], ACT.Copy,
                             scale=gwT[:, bass.ds(e, 1)]).then_inc(y_ok, 1)

            act.wait_ge(bias_zero, 1)

            def one_pass(r):
                E0, X0, n0, w0 = r * NE, r * (NE + 1), r * PASS, r * (16 * PASS // XRAW)
                select(0, sel_gu, selg_ok, gub_pe, E0)
                high_x(n0, w0, N0 + 2)
                rows_high(X0)
                for c in range(GUC):
                    if c >= 3:
                        high_x(n0, w0, N0 + c)
                    if c == 3:
                        select(1, sel_gu, selg_ok, gub_pe, E0 + 1)
                rows_high(X0 + 1)
                sigmoid(E0, 0)
                sigmoid(E0, 1)
                high_x(n0, w0, N0 + GUC)
                high_x(n0, w0, N0 + GUC + 1)
                hidden_high(E0)
                with act.Fori(1, NE) as e:
                    E, X = E0 + e, X0 + e
                    ne, we = n0 + e * EC, w0 + e * (16 * EC // XRAW)
                    for c in range(2, EC + 2):
                        high_x(ne, we, N0 + GUC - EC + c)
                        if c == 3:
                            select(e + 1, sel_gu, selg_ok, gub_pe, E + 1)
                        if c == 5:
                            select(e - 1, sel_dn, seld_ok, dnb_pe, E - 1)
                        if c == 10:
                            rows_high(X + 1)
                            sigmoid(E, 0)
                        if c == 11:
                            sigmoid(E, 1)
                    hidden_high(E)
                    weighted(E - 1, e - 1)
                select(NE - 1, sel_dn, seld_ok, dnb_pe, E0 + (NE - 1))
                high_x(n0, w0, N0 + PASS - 2)
                high_x(n0, w0, N0 + PASS - 1)
                act.wait_ge(split_used, n0 + (N0 + PASS))
                weighted(E0 + (NE - 1), NE - 1)

            act.wait_ge(h2_out, 16 * NT)
            one_pass(0)
            more_passes(act, lambda r: (presplit(r * PASS, r * (16 * PASS // XRAW)), one_pass(r)))
            for j in range(NT):
                act.wait_ge(fin_in[j], 16)
                if j:
                    act.wait_ge(fsq_ok, j)
                S.activation(fsq[:, :], fin[:, j, :], ACT.Square, accum_out=ss[:, 16 + j:17 + j]).then_inc(fsq_ok, 1)

        @block.vector
        def _(dve):
            Vv = nc.vector
            link = Chain(dve, dve_own)

            def low(n):
                dve.wait_ge(hi_done, n + 1)
                w = block_of(n)[1]
                Vv.tensor_tensor(wlo[:, n % SPL, 0:w], raw[:, n % RAW, 0:w], whi[:, n % SPL, 0:w], ALU.subtract).then_inc(lo_dve, 1)

            for j in range(NT):
                dve.wait_ge(x_rms, j + 1)
                Vv.tensor_scalar(xnat[:, j, :], xnat[:, j, :], rstd[:, j:j + 1], None, ALU.mult).then_inc(xs_ok, 1)
            low(0)
            low(1)
            for k in range(KD):
                dve.wait_ge(hT_hi_ok, k + 1)
                Vv.scalar_tensor_tensor(out=actT_lo[:, k, :], in0=ps[:, k, :], scalar=vecT[:, k:k + 1],
                                        in1=actT_hi[:, k, :], op0=ALU.mult, op1=ALU.subtract).then_inc(hT_lo_ok, 1)
            low(2)
            dve.wait_ge(pos_in, 32)
            link(Vv.tensor_copy(posf[:, :], posi[:, :]))
            link(Vv.tensor_scalar(posf[:, :], posf[:, :], frq[:, 0:1], None, ALU.mult))
            for dst, shift in ((ang, 0.25), (angk, 0.0)):
                turns = acc2[:, 0, :]
                link(Vv.tensor_scalar(turns, posf[:, :], 1.0 / TWO_PI, shift, ALU.mult, ALU.add))
                link(Vv.tensor_scalar(turns, turns, MAGIC, None, ALU.add))
                link(Vv.tensor_scalar(turns, turns, MAGIC, None, ALU.subtract))
                link(Vv.scalar_tensor_tensor(out=dst[:, :], in0=turns, scalar=-C1, in1=posf[:, :], op0=ALU.mult, op1=ALU.add))
                link(Vv.scalar_tensor_tensor(out=dst[:, :], in0=turns, scalar=-C2, in1=dst[:, :], op0=ALU.mult, op1=ALU.add))
                link(Vv.scalar_tensor_tensor(out=dst[:, :], in0=turns, scalar=-C3, in1=dst[:, :], op0=ALU.mult, op1=ALU.add))
                if shift:
                    link(Vv.tensor_scalar(dst[:, :], dst[:, :], shift * TWO_PI, None, ALU.add))
                Vv.tensor_scalar(dst[:, :], dst[:, :], 3.141592, -3.141592, ALU.min, ALU.max).then_inc(trig_in, 1)
            low(3)
            low(4)
            dve.wait_ge(lat_sq, 2 * NT)
            dve.wait_ge(par_in, 48)
            Vv.tensor_tensor(dt[:, :, :], ps[:, 0:4, 0:8], dtb[:, :].unsqueeze(1).to_broadcast([P, NT, HEADS]), ALU.add).then_inc(dt_in, 1)
            kr0 = 8 + QR + KVR
            Vv.tensor_copy(krn[:, :, 0, :], ps[:, 0:4, kr0:kr0 + ROPE])
            Vv.tensor_copy(krn[:, :, 1, 0:ROPE // 2], ps[:, 0:4, kr0 + ROPE // 2:kr0 + ROPE])
            Vv.tensor_copy(krn[:, :, 1, ROPE // 2:ROPE], ps[:, 0:4, kr0:kr0 + ROPE // 2])
            dve.wait_ge(lat_rms, 2)
            for j in range(NT):
                Vv.tensor_scalar(latn[:, j, 0:QR], ps[:, j, 8:8 + QR], rstd[:, 4 + j:5 + j], None, ALU.mult)
                Vv.tensor_scalar(latn[:, j, QR:QR + KVR], ps[:, j, 8 + QR:kr0], rstd[:, 8 + j:9 + j], None, ALU.mult).then_inc(lat_ok, 1)
            dve.wait_ge(dt_e, 3)
            link(Vv.scalar_tensor_tensor(out=dt[:, :, :], in0=dt[:, :, :], scalar=0.0, in1=dtx[:, :, :], op0=ALU.max, op1=ALU.add))
            Vv.scalar_tensor_tensor(out=adt[:, :, :], in0=dt[:, :, :], scalar=-1.0,
                                    in1=alog[:, :].unsqueeze(1).to_broadcast([P, NT, HEADS]),
                                    op0=ALU.mult, op1=ALU.mult).then_inc(adt_ok, 1)
            low(5)

            def conv(m):
                dve.wait_ge(u_ok, m + 1)
                if m >= 2:
                    dve.wait_ge(xbc_ok, m - 1)
                a, u = acc2[:, m % 2, :], U[:, m % 4, :]
                tap = lambda q: vecT[:, 8 + 8 * q + m:9 + 8 * q + m]
                link(Vv.tensor_scalar(a, u[:, 0:SEQ], tap(0), None, ALU.mult))
                for q in range(1, 4):
                    ins = Vv.scalar_tensor_tensor(out=a, in0=u[:, q:q + SEQ], scalar=tap(q), in1=a, op0=ALU.mult, op1=ALU.add)
                    if q < 3:
                        link(ins)
                ins.then_inc(conv_ok, 1)

            dve.wait_ge(pad_ok, 1)
            for m in range(4):
                conv(m)
                if m == 1:
                    low(6)
            low(7)
            for m in range(4, 8):
                conv(m)
                if m == 5:
                    low(8)

            dve.wait_ge(trig_ok, 1)
            dve.wait_ge(xbc_ok, 8)
            for i, (kind, a, eng) in enumerate(MLA):
                if eng != "D":
                    continue
                b = i % 8
                dve.wait_ge(mla_pe, i + 1)
                if kind == "lat":
                    Vv.tensor_scalar(cqT[:, a, :], ps[:, b, :], vecT[:, 48 + a:49 + a], None, ALU.mult).then_inc(mla_dve, 1)
                elif kind == "kr":
                    dst, tab = ((ropeS, COS), (ropeR, SIN))[a]
                    Vv.tensor_tensor(dst[0:ROPE, :], ps[0:ROPE, b, :], tab[0:ROPE, :], ALU.mult).then_inc(mla_dve, 1)
                    if a == 1:
                        mla_evacuated(dve, i)
                        Vv.tensor_tensor(krf[:, :], ropeS[0:ROPE, :], ropeR[0:ROPE, :], ALU.add).then_inc(kr_sum, 1)
                        dve.wait_ge(kr_sum, 1)
                        for h in range(4):
                            ins = Vv.tensor_copy(KT[NOPE:QK, h, :], krf[:, :])
                        ins.then_inc(kr_dve, 1)
                elif kind in ("qn", "kn"):
                    dst = QT if kind == "qn" else KT
                    Vv.tensor_copy(dst[0:NOPE, 2 * a, :], ps[0:NOPE, b, :])
                    Vv.tensor_copy(dst[0:NOPE, 2 * a + 1, :], ps[NOPE:P, b, :]).then_inc(mla_dve, 1)
                elif kind == "qs":
                    mla_evacuated(dve, i - 1)
                    dve.wait_ge(kr_dve, 1)
                    Vv.tensor_tensor(ropeS[:, :], ps[:, b, :], COS[:, :], ALU.mult).then_inc(mla_dve, 1)
                elif kind == "qr":
                    link(Vv.tensor_tensor(ropeR[:, :], ps[:, b, :], SIN[:, :], ALU.mult))
                    for q in range(4):
                        rows = slice(q * ROPE, (q + 1) * ROPE)
                        ins = Vv.tensor_tensor(QT[NOPE:QK, 4 * a + q, :], ropeS[rows, :], ropeR[rows, :], ALU.add)
                    ins.then_inc(mla_dve, 1)
                else:
                    Vv.tensor_copy(V[:, a, :], ps[:, b, :]).then_inc(mla_dve, 1)

            def attended(m):
                dve.wait_ge(yatt_hi, m + 1)
                Vv.tensor_tensor(actT_lo[:, slot_of(4 + m), :], ps[:, 4 + m % 2, :], actT_hi[:, slot_of(4 + m), :],
                                 ALU.subtract).then_inc(yatt_lo, 1)

            def normalise(u):
                w = (u % NT + 1) * P
                dve.wait_ge(exp_done, u + 1)
                link(Vv.reciprocal(rsum[:, u:u + 1], rsum[:, u:u + 1]))
                Vv.tensor_scalar(Pr[:, u % 4, 0:w], Pr[:, u % 4, 0:w], rsum[:, u:u + 1], None, ALU.mult).then_inc(pn_done, 1)

            for u in range(NU):
                dve.wait_ge(s_done, u + 1)
                Vv.tensor_reduce(nmax[:, u:u + 1], ps[:, S_BANK[u % 4], 0:(u % NT + 1) * P], AX, ALU.min).then_inc(nm_done, 1)
                if u >= 1:
                    normalise(u - 1)
                if u % 8 == 6 and u > 8:
                    attended(u // 8 - 1)
                if u in (9, 17):
                    low(9 + u // 16)
            normalise(NU - 1)
            attended(HEADS // 2 - 1)

            fl = lambda t: t[:, :, :].rearrange("p j h -> p (j h)")
            dve.wait_ge(cum_pe, 1)
            Vv.tensor_scalar(fl(nacum), ps[:, 7, 0:32], -1.0, None, ALU.mult).then_inc(cum_dve, 1)
            dve.wait_ge(cum_dve, 1)
            Vv.tensor_tensor(fl(dtx), ps[:, 7, 32:64], fl(nacum), ALU.add).then_inc(cum_dve, 1)
            dve.wait_ge(cum_act, 3)
            by_head = lambda t: t.rearrange("p (h d) -> p h d", h=HEADS)
            for j in range(NT):
                dve.wait_ge(bn_ok, j + 1)
                if j >= 1:
                    dve.wait_ge(yd_pe, j)
                for g in range(GROUPS):
                    dve.wait_ge(dm_ok, 2 * j + g + 1)
                    Vv.tensor_tensor(Mm[:, g, :, :], Dm[:, g, :, :],
                                     ps[:, 1, (2 + g) * P:(3 + g) * P].unsqueeze(1).to_broadcast([P, 4, P]),
                                     ALU.mult).then_inc(mm_ok, 1)
                if j < NT - 1:
                    dve.wait_ge(st_pe, j + 1)
                    if j == 0:
                        Vv.tensor_copy(hst[:, :], ps[:, 7, :]).then_inc(h_ok, 1)
                    else:
                        dve.wait_ge(hm_ok, j)
                        dve.wait_ge(yo_pe, j)
                        Vv.tensor_tensor(hst[:, :], htmp[:, :], ps[:, 7, :], ALU.add).then_inc(h_ok, 1)
                dve.wait_ge(yd_pe, j + 1)
                if j == 0:
                    dve.wait_ge(sz_ok, NT)
                    Vv.tensor_copy(yt[:, :], ps[:, 4, :]).then_inc(y1_ok, 1)
                else:
                    dve.wait_ge(y2_ok, j)
                    dve.wait_ge(yo_pe, j)
                    link(Vv.tensor_tensor(by_head(yt[:, :]), by_head(ps[:, 6, :]), heads(eacum[:, j, :], HD), ALU.mult))
                    Vv.tensor_tensor(yt[:, :], yt[:, :], ps[:, 4 + j % 2, :], ALU.add).then_inc(y1_ok, 1)
                dve.wait_ge(y1_ok, j + 1)
                dve.wait_ge(ydx_ok, j + 1)
                link(Vv.tensor_tensor(yt[:, :], yt[:, :], ydx[:, :], ALU.add))
                Vv.tensor_tensor(Ynat[:, j, 0:SSDW], yt[:, :], sz[:, j, :], ALU.mult).then_inc(y2_ok, 1)

            for f in range(4):
                dve.wait_ge(yT_hi, f + 1)
                Vv.scalar_tensor_tensor(out=actT_lo[:, slot_of(f), :], in0=ps[:, 6 + f % 2, :], scalar=vecT[:, 51 + f:52 + f],
                                        in1=actT_hi[:, slot_of(f), :], op0=ALU.mult, op1=ALU.subtract).then_inc(yT_lo, 1)
            low(11)
            dve.wait_ge(bias_hi, 1)
            dve.wait_ge(bias_zero, 1)
            Vv.tensor_tensor(biasB[32:64, :], biasR[32:64, :], biasB[32:64, :], ALU.subtract).then_inc(bias_lo, 1)
            def low_x(n0, k):
                dve.wait_ge(hi_done, n0 + (k + 1))
                Vv.tensor_tensor(wlo[:, k % SPL, 0:DVE_COLS], xraw(k)[:, 0:DVE_COLS], whi[:, k % SPL, 0:DVE_COLS],
                                 ALU.subtract).then_inc(lo_dve, 1)

            def presplit(n0):
                low_x(n0, N0)
                low_x(n0, N0 + 1)

            presplit(0)

            def residual(j):
                if j < NT - 1:
                    dve.wait_ge(x2_pe, j + 1)
                else:
                    dve.wait_ge(split_used, N0)
                Vv.tensor_tensor(x2[:, j, :].rearrange("p (a n) -> p a n", a=2), ps[:, 2 * j:2 * j + 2, :],
                                 x2[:, j, :].rearrange("p (a n) -> p a n", a=2), ALU.add).then_inc(x2_ok, 1)

            dve.wait_ge(xr_in, 64)
            dve.wait_ge(gn_in, 32)
            residual(0)
            for j in range(NT):
                if j < NT - 1:
                    residual(j + 1)
                dve.wait_ge(x2_rms, j + 1)
                Vv.scalar_tensor_tensor(out=h2[:, j, :], in0=x2[:, j, :], scalar=rstd[:, 12 + j:13 + j], in1=gffn[:, :],
                                        op0=ALU.mult, op1=ALU.mult).then_inc(h2_ok, 1)
            over_k = lambda t: t[:, :, :].rearrange("p (j k) e -> p j e k", k=TOPK)
            dve.wait_ge(iota_ok, 2)
            for j in range(NT):
                mine = slice(j * TOPK, (j + 1) * TOPK)
                dve.wait_ge(lg_pe, j + 1)
                link(Vv.tensor_tensor(lgt[:, j, :], ps[:, 2 * j, 0:NE], brt[:, :], ALU.add))
                link(Vv.max(top8[:, j, :], lgt[:, j, :]))
                link(Vv.max_index(topi[:, j, :], top8[:, j, :], lgt[:, j, :]))
                link(Vv.tensor_copy(topf[:, j, :], topi[:, j, 0:TOPK]))
                link(Vv.tensor_tensor(eq[:, mine, :], iota_f[:, 0:NE].unsqueeze(1).to_broadcast([P, TOPK, NE]),
                                      topf[:, j, :].unsqueeze(2).to_broadcast([P, TOPK, NE]), ALU.is_equal))
                link(Vv.tensor_reduce(mask[:, j, :], eq[:, mine, :].rearrange("p k e -> p e k"), AX, ALU.add))
                ins = Vv.tensor_copy(maskb[:, j, :], mask[:, j, :])
                if j < NT - 1:
                    link(ins)
            ins.then_inc(mask_ok, 1)
            Vv.tensor_tensor(gate[:, :, :], top8[:, :, 0:TOPK], top8[:, :, 0:1].to_broadcast([P, NT, TOPK]), ALU.subtract).then_inc(ge_in, 1)
            dve.wait_ge(ge_ok, 1)
            link(Vv.tensor_reduce(gsum[:, :], gate[:, :, :], AX, ALU.add))
            link(Vv.reciprocal(gsum[:, :], gsum[:, :]))
            link(Vv.tensor_tensor(gate[:, :, :], gate[:, :, :], gsum[:, :].unsqueeze(2).to_broadcast([P, NT, TOPK]), ALU.mult))
            link(Vv.tensor_tensor(eqg[:, :, :], eq[:, :, :], 
                                  gate[:, :, :].rearrange("p j k -> p (j k)").unsqueeze(2).to_broadcast([P, NT * TOPK, NE]), ALU.mult))
            dve.wait_ge(tg_ok, 2)
            link(Vv.tensor_reduce(gsc[:, :, :], over_k(eqg), AX, ALU.add))
            for q in range(3):
                link(Vv.tensor_copy(TG[:, :, 0:NE, 3 + q], gsc[:, :, :]))
                if q < 2:
                    link(Vv.tensor_tensor(gsc[:, :, :], gsc[:, :, :], TG[:, :, 0:NE, 3 + q], ALU.subtract))
            dve.wait_ge(rank_pe, 1)
            dve.wait_ge(mask_ok, 1)
            dve.wait_ge(iota_ok, 2)
            link(Vv.scalar_tensor_tensor(out=rank[:, :, 0:NE], in0=ps[:, 1, 0:NT * NE].rearrange("p (j e) -> p j e", j=NT),
                                         scalar=1.0, in1=mask[:, :, :], op0=ALU.add, op1=ALU.mult))
            link(Vv.tensor_scalar(rank[:, :, 0:NE], rank[:, :, 0:NE], -1.0, None, ALU.add))
            link(Vv.reduce_max(cntf[:, 0:1], ps[:, 3, 0:NE], AX))
            Vv.tensor_copy(cnti[:, 0:1], cntf[:, 0:1]).then_inc(route_ok, 1)

            both = lambda t: t[:, :, :].rearrange("p (a k) n -> p a (k n)", a=2)

            def places(D, e):
                dve.wait_ge(disp_pe, past(D))
                Vv.tensor_tensor(onehot[:, :, :], iota_f[:, :].unsqueeze(1).to_broadcast([P, NT, P]),
                                 rank[:, :, bass.ds(e, 1)].to_broadcast([P, NT, P]), ALU.is_equal).then_inc(oh_ok, 1)

            def table(D, e, bank=6, first=False):
                dve.wait_ge(disp_pe, past(D + 1))
                if not first:
                    dve.wait_ge(x_got, 16 * D)
                Vv.tensor_reduce(gwT[:, bass.ds(e, 1)], ps[:, bank, 3:6], AX, ALU.add)
                Vv.tensor_reduce(idx_f[:, :], ps[:, bank, 0:2], AX, ALU.add).then_inc(disp_t, 1)
                dve.wait_ge(disp_t, 2 * D + 1)
                Vv.scalar_tensor_tensor(out=idx_f[:, :], in0=ps[:, bank, 2:3], scalar=smid[:, 0:1], in1=idx_f[:, :],
                                        op0=ALU.mult, op1=ALU.add).then_inc(disp_t, 1)
                dve.wait_ge(disp_t, 2 * D + 2)
                Vv.tensor_scalar(idxT[:, bass.ds(e, 1)], idx_f[:, :], smid[:, 1:2], None, ALU.add)
                Vv.tensor_scalar(idx_g[:, :], idx_f[:, :], smid[:, 1:2], None, ALU.add).then_inc(idx_ok, 1)

            def rows_low(X):
                dve.wait_ge(xt_hi, X + 1)
                Vv.tensor_tensor(both(XT_lo), ps[:, 6:8, :], both(XT_hi), ALU.subtract).then_inc(xt_lo, 1)

            def hidden_low(E):
                dve.wait_ge(ht_hi, past(E + 1))
                Vv.tensor_tensor(both(HT_lo), ps[:, 6:8, :], both(HT_hi), ALU.subtract).then_inc(ht_lo, 1)

            def clamp(E, done):
                dve.wait_ge(split_used, done)
                for f in range(2):
                    Vv.tensor_scalar(gc[:, f, :], ps[:, f, :], LIMIT, None, ALU.min).then_inc(gc_ok, 1)
                    Vv.tensor_scalar(uc[:, f, :], ps[:, 2 + f, :], LIMIT, -LIMIT, ALU.min, ALU.max).then_inc(uc_ok, 1)

            def hidden(E):
                dve.wait_ge(uc_ok, past(2 * E + 2))
                dve.wait_ge(gc_ok, 2 * E + 2)
                for f in range(2):
                    Vv.scalar_tensor_tensor(out=uc[:, f, :], in0=uc[:, f, :], scalar=1.0, in1=gc[:, f, :],
                                            op0=ALU.add, op1=ALU.mult).then_inc(t_ok, 1)
                dve.wait_ge(t_ok, 2 * E + 2)
                for f in range(2):
                    dve.wait_ge(sg_ok, 2 * E + (f + 1))
                    Vv.tensor_tensor(uc[:, f, :], uc[:, f, :], sg[:, f, :], ALU.mult).then_inc(h_act, 1)

            def one_pass(r):
                E0, X0, D0, n0 = r * NE, r * (NE + 1), r * PADE, r * PASS
                dve.wait_ge(rank_ok, past(r))
                places(D0, 0)
                table(D0, 0, bank=6, first=True)
                places(D0 + 1, 1)
                low_x(n0, N0 + 2)
                rows_low(X0)
                table(D0 + 1, 1, bank=5)
                for c in range(GUC):
                    if c >= 3:
                        low_x(n0, N0 + c)
                    if c == 2:
                        places(D0 + 2, 2)
                    if c == 5:
                        table(D0 + 2, 2)
                rows_low(X0 + 1)
                clamp(E0, n0 + (N0 + GUC))
                hidden(E0)
                low_x(n0, N0 + GUC)
                low_x(n0, N0 + GUC + 1)
                hidden_low(E0)
                with dve.Fori(1, NE) as e:
                    E, X, D, ne = E0 + e, X0 + e, D0 + e, n0 + e * EC
                    for c in range(2, EC + 2):
                        low_x(ne, N0 + GUC - EC + c)
                        if c == 2:
                            places(D + 2, e + 2)
                        if c == 5:
                            table(D + 2, e + 2)
                        if c == 10:
                            rows_low(X + 1)
                            clamp(E, ne + (N0 + 2 * GUC - EC))
                        if c == 11:
                            hidden(E)
                    hidden_low(E)
                low_x(n0, N0 + PASS - 2)
                low_x(n0, N0 + PASS - 1)
                dve.wait_ge(oh_ok, D0 + PADE)
                dve.wait_ge(x_got, 16 * (D0 + PADE))
                Vv.tensor_scalar(rank[:, :, :], rank[:, :, :], -float(P), None, ALU.add).then_inc(rank_ok, 1)

            dve.wait_ge(h2_out, 16 * NT)
            one_pass(0)
            more_passes(dve, lambda r: (presplit(r * PASS), one_pass(r)))
            for j in range(NT):
                dve.wait_ge(f_rms, j + 1)
                Vv.scalar_tensor_tensor(out=fin[:, j, :], in0=fin[:, j, :], scalar=rstd[:, 16 + j:17 + j], in1=gfin[:, :],
                                        op0=ALU.mult, op1=ALU.mult).then_inc(fo_ok, 1)

        @block.gpsimd
        def _(pool):
            G = nc.gpsimd
            link = Chain(pool, pool_own)

            def keep(t, cmp, fill, base, step, per_row, cols=P):
                return G.affine_select(out=t, in_=t, compare_op=cmp, fill=fill, base=base, pattern=[[step, cols]],
                                       channel_multiplier=per_row)

            for s in (gub_pe, dnb_pe, disp_pe, xt_pe, ht_hi, ht_lo, uc_ok, y_ok, rank_ok):
                pool.sem_inc(s, past(0))
            G.memset(Uinc[:, :], 1.0)
            G.memset(onesf[:, :], 1.0)
            G.memset(onesb[:, :], 1.0)
            G.memset(mhalf[:, :], -0.5)
            G.memset(identb[:, :], 0.0)
            G.memset(maskA[:, :], 0.0)
            G.memset(maskS[:, :], 0.0)
            G.memset(esel[:, :], 0.0)
            link(G.memset(ident[:, :], 0.0))
            keep(ident[:, :], ALU.not_equal, 1.0, 0, -1, 1).then_inc(konst_ok, 1)
            keep(Uinc[:, :], ALU.is_ge, 0.0, 0, 1, -1)
            keep(identb[:, :], ALU.not_equal, 1.0, 0, -1, 1)
            keep(maskA[:, :], ALU.is_ge, -NEG, 0, -1, 1)
            keep(maskS[:, :], ALU.is_ge, NEG, 0, 1, -1)
            link(keep(esel[:, :], ALU.not_equal, 1.0, 0, -1, 1, PADE))
            link(keep(esel[:, :], ALU.not_equal, 1.0, -32, -1, 1, PADE))
            link(G.iota(kint[:, :], pattern=[[1, P]], base=0, channel_multiplier=0))
            link(G.tensor_copy(iota_f[:, :], kint[:, :]))
            link(G.iota(kint[:, 0:1], pattern=[[1, 1]], base=0, channel_multiplier=1))
            link(G.tensor_copy(smid[:, 3:4], kint[:, 0:1]))
            G.tensor_scalar(smid[:, 0:1], smid[:, 3:4], -1.0, 0.0, ALU.mult, ALU.add)
            G.tensor_scalar(smid[:, 1:2], smid[:, 3:4], 1.0, float(TRASH), ALU.mult, ALU.add)
            G.tensor_scalar(smid[:, 2:3], smid[:, 3:4], 1.0, -float(SEQ), ALU.mult, ALU.add).then_inc(iota_ok, 2)
            G.memset(U[:, :, 0:3], 0.0).then_inc(pad_ok, 1)

            def low(n):
                pool.wait_ge(hi_done, n + 1)
                w, d = block_of(n)
                G.tensor_tensor(wlo[:, n % SPL, d:w], raw[:, n % RAW, d:w], whi[:, n % SPL, d:w], ALU.subtract).then_inc(lo_pool, 1)

            def inv_rms(c, n, width):
                link(G.tensor_scalar(rstd[:, c:c + n], ss[:, c:c + n], 1.0 / width, EPS, ALU.mult, ALU.add))
                return G.tensor_tensor(rstd[:, c:c + n], rstd[:, c:c + n], mhalf[:, 0:n], ALU.pow)

            for j in range(NT):
                pool.wait_ge(xsq, j + 1)
                inv_rms(j, 1, DM).then_inc(x_rms, 1)
            for n in range(5):
                low(n)
            pool.wait_ge(lat_sq, 2 * NT)
            inv_rms(4, 4, QR).then_inc(lat_rms, 1)
            inv_rms(8, 4, KVR).then_inc(lat_rms, 1)
            for n in range(5, 11):
                low(n)

            by_head = lambda t: t.rearrange("p (h d) -> p h d", h=HEADS)

            def y_norm(j):
                pool.wait_ge(ysq, 2 * j + 2)
                inv_rms(20 + 2 * j, 2, 256).then_inc(y_rms, 1)

            pool.wait_ge(par_in, 48)
            for j in range(NT):
                pool.wait_ge(xn_ok, j + 1)
                if j == 0:
                    pool.wait_ge(cum_act, 3)
                if j >= 2:
                    pool.wait_ge(yd_pe, j - 1)
                    pool.wait_ge(st_pe, j - 1)
                G.tensor_tensor(by_head(xd[:, j % 2, :]), by_head(Xn[:, j, :]), heads(dt[:, j, :], HD), ALU.mult).then_inc(xd_ok, 1)
                if j < NT - 1:
                    pool.wait_ge(xd_ok, j + 1)
                    G.tensor_tensor(by_head(xdd[:, j % 2, :]), by_head(xd[:, j % 2, :]), heads(dte[:, j, :], HD), ALU.mult).then_inc(xdd_ok, 1)
                    if j >= 1:
                        pool.wait_ge(h_ok, j)
                        G.tensor_tensor(by_head(htmp[:, :]), by_head(hst[:, :]), heads(cdec[:, j, :], HD), ALU.mult).then_inc(hm_ok, 1)
                if j >= 1:
                    pool.wait_ge(y2_ok, j)
                G.tensor_tensor(by_head(ydx[:, :]), by_head(Xn[:, j, :]), heads(dsk[:, :], HD), ALU.mult).then_inc(ydx_ok, 1)
                if j >= 1:
                    y_norm(j - 1)
            y_norm(NT - 1)

            pool.wait_ge(yssd, NT)
            for j in range(NT):
                pool.dma_start(x2[:, j, :], A["x"][0, j * P:(j + 1) * P, :]).then_inc(xr_in, 16)
            pool.dma_start(gffn[:, :], A["norm_ffn_g"][0].partition_broadcast(P)).then_inc(gn_in, 16)
            pool.dma_start(gfin[:, :], A["norm_final_g"].partition_broadcast(P)).then_inc(gn_in, 16)
            for q in range(2):
                rows = slice(32 * q, 32 * q + NE)
                pool.dma_start(biasR[rows, 0:2 * DFF], A["b_gate_up"][0]).then_inc(bias_in, 16)
                pool.dma_start(biasR[rows, 2 * DFF:3 * DFF], A["b_down"][0]).then_inc(bias_in, 16)
            G.memset(biasB[64:P, :].bitcast(F32), 0.0).then_inc(bias_zero, 1)
            pool.wait_ge(bias_zero, 1)
            link(G.memset(Ustrict[:, :], 1.0))
            keep(Ustrict[:, :], ALU.is_gt, 0.0, 0, 1, -1).then_inc(tg_ok, 1)
            G.memset(rank[:, :, NE:PADE], -1.0)
            link(G.memset(TG[:, :, :, :], 0.0))
            pool.wait_ge(iota_ok, 2)
            G.tensor_scalar(TG[:, :, :, 2], TG[:, :, :, 2], 1.0, 1.0, ALU.mult, ALU.add)
            G.tensor_scalar(TG[:, :, :, 0], TG[:, :, :, 0], smid[:, 3:4], 0.0, ALU.add, ALU.add)
            for j in range(NT):
                ins = G.memset(TG[:, j, :, 1], float(j * P - SEQ))
            ins.then_inc(tg_ok, 1)
            def low_x(n0, k):
                pool.wait_ge(hi_done, n0 + (k + 1))
                G.tensor_tensor(wlo[:, k % SPL, DVE_COLS:], xraw(k)[:, DVE_COLS:], whi[:, k % SPL, DVE_COLS:],
                                ALU.subtract).then_inc(lo_pool, 1)

            def presplit(n0):
                low_x(n0, N0)
                low_x(n0, N0 + 1)

            low(11)
            presplit(0)
            for j in range(NT):
                pool.wait_ge(x2sq, j + 1)
                inv_rms(12 + j, 1, DM).then_inc(x2_rms, 1)
            pool.wait_ge(split_used, N0)
            link(G.memset(Xg[:, :], 0.0))
            pool.dma_start(acc_d[SEQ:SEQ + P, :], Xg[:, :]).then_inc(y_added, 16 * past(0))
            pool.wait_ge(y_added, 16 * past(0))
            pool.wait_ge(acc_out, 16 * NT)
            pool.wait_ge(h2_out, 16 * NT)

            def gather(D, X):
                pool.wait_ge(idx_ok, D + 1)
                pool.wait_ge(xt_pe, past(X))
                pool.sem_inc(rows_asked, 1)
                G.indirect_dma_start(Xg[:, :], None, h2_d, bass.IndirectOffsetOnAxis(idx_g[:, 0:1], 0),
                                     bounds_check=SEQ - 1, oob_is_err=False).then_inc(x_got, 16)

            def scatter(E, e):
                pool.wait_ge(y_ok, past(E + 1))
                pool.sem_inc(rows_sent, 1)
                G.indirect_dma_start(acc_d, bass.IndirectOffsetOnAxis(idx_s[:, 0:1], 0), ysb[:, :], None,
                                     compute_op=ALU.add).then_inc(y_added, 16)

            def one_pass(r):
                E0, X0, D0, n0 = r * NE, r * (NE + 1), r * PADE, r * PASS
                gather(D0, X0)
                gather(D0 + 1, X0 + 1)
                for c in range(2, GUC + 2):
                    low_x(n0, N0 + c)
                gather(D0 + 2, X0 + 2)
                with pool.Fori(1, NE) as e:
                    E, X, D, ne = E0 + e, X0 + e, D0 + e, n0 + e * EC
                    for c in range(2, EC + 2):
                        low_x(ne, N0 + GUC - EC + c)
                        if c == 11:
                            gather(D + 2, X + 2)
                    scatter(E - 1, e - 1)
                low_x(n0, N0 + PASS - 2)
                low_x(n0, N0 + PASS - 1)
                scatter(E0 + (NE - 1), NE - 1)
                pool.wait_ge(y_added, 16 * past(E0 + NE))

            one_pass(0)
            more_passes(pool, lambda r: (presplit(r * PASS), one_pass(r)))
            pool.sem_inc(all_added, 1)
            for j in range(NT):
                pool.wait_ge(fsq_ok, j + 1)
                inv_rms(16 + j, 1, DM).then_inc(f_rms, 1)


_INS = ['x', 'positions', 'norm_mix_g', 'w_in', 'conv_w', 'conv_b', 'dt_bias', 'a_log', 'd_skip', 'ssd_norm_g',
        'q_norm_g', 'w_uq', 'kv_norm_g', 'w_ukv', 'w_out', 'norm_ffn_g', 'w_router', 'b_router',
        'w_gate_up', 'b_gate_up', 'w_down', 'b_down', 'norm_final_g']


def kernel(**inputs):
    import concourse.bacc as bacc
    from concourse.bass_utils import run_bass_kernel_spmd

    nc = bacc.Bacc("TRN2", target_bir_lowering=False, num_devices=1)
    half = np.arange(P) % (ROPE // 2)
    freq = np.power(np.float32(10000.0), -(2 * half).astype(np.float32) / np.float32(ROPE)).astype(np.float32)
    sign = np.where(np.arange(P) % ROPE < ROPE // 2, -1.0, 1.0).astype(np.float32)
    arrays, args = {}, {}
    for name in _INS + ['rope_freq']:
        a = np.stack([freq, sign], axis=1) if name == 'rope_freq' else np.ascontiguousarray(inputs[name])
        arrays[f"in_{name}_dram"] = a
        args[name] = nc.dram_tensor(f"in_{name}_dram", a.shape, mybir.dt.from_np(a.dtype), kind="ExternalInput").ap()
    out = nc.dram_tensor("out_0_dram", (1, SEQ, DM), F32, kind="ExternalOutput").ap()
    layer(nc, args, out)
    r = run_bass_kernel_spmd(nc, [arrays], core_ids=[0])
    return r.results[0]["out_0_dram"]
```
